# Optimizing a Trainium2 kernel written in Bass

```python
import math
import jax, jax.numpy as jnp
from jax import lax
import numpy as np

D_MODEL = 1024
BATCH = 1
SEQ = 256
DEPTH = 2

N_A = DEPTH // 2
N_B = DEPTH - N_A

GLA_HEADS = 4
GLA_DK = (D_MODEL // 2) // GLA_HEADS
GLA_DV = D_MODEL // GLA_HEADS
GLA_GATE_RANK = 16
GLA_TAU = 16.0
GLA_CHUNK = 64
GLA_COLS = (GLA_HEADS * GLA_DK, GLA_HEADS * GLA_DK, GLA_HEADS * GLA_DV, GLA_HEADS * GLA_DV, GLA_GATE_RANK)
GLA_SPLITS = list(np.cumsum(GLA_COLS)[:-1].tolist())
GLA_IN = int(sum(GLA_COLS))

DIFF_HEADS = 8
DIFF_DH = 64
DIFF_VD = 2 * DIFF_DH
Q_BLOCK = 128

MLP_HIDDEN = 4 * D_MODEL
NORM_EPS = 1e-6


def rms_norm(x, g):
    xf = x.astype(jnp.float32)
    y = xf * lax.rsqrt(jnp.mean(xf * xf, axis=-1, keepdims=True) + NORM_EPS)
    return (y * g.astype(jnp.float32)).astype(x.dtype)

def sqrelu_mlp(xn, w1, w2):
    return jnp.square(jax.nn.relu(xn @ w1)) @ w2

def gla_chunked(q, k, v, log_a):
    B, S, H, DK = q.shape
    DV = v.shape[-1]
    C = GLA_CHUNK
    n = S // C

    def chunks(t):
        return t.astype(jnp.float32).reshape(B, n, C, H, t.shape[-1]).transpose(1, 0, 3, 2, 4)

    qc = chunks(q) * (DK ** -0.5)
    kc = chunks(k)
    vc = chunks(v)
    bc = jnp.cumsum(chunks(log_a), axis=-2)
    causal = jnp.tril(jnp.ones((C, C), bool))

    def step(state, inp):
        qi, ki, vi, bi = inp
        diff = bi[:, :, :, None, :] - bi[:, :, None, :, :]
        decay = jnp.exp(jnp.where(causal[:, :, None], diff, -jnp.inf))
        attn = jnp.einsum('bhid,bhjd,bhijd->bhij', qi, ki, decay)
        o = (jnp.einsum('bhij,bhjv->bhiv', attn, vi)
             + jnp.einsum('bhid,bhdv->bhiv', qi * jnp.exp(bi), state))
        b_last = bi[:, :, -1:, :]
        state = (jnp.exp(b_last[:, :, 0, :, None]) * state
                 + jnp.einsum('bhjd,bhjv->bhdv', ki * jnp.exp(b_last - bi), vi))
        return state, o

    _, o = lax.scan(step, jnp.zeros((B, H, DK, DV), jnp.float32), (qc, kc, vc, bc))
    return o.transpose(1, 0, 3, 2, 4).reshape(B, S, H, DV)

def gla_mixer(xn, w_in, w_gate_up, b_gate, head_gain, w_out):
    B, S, _ = xn.shape
    proj = xn @ w_in
    q, k, v, g, z = jnp.split(proj, GLA_SPLITS, axis=-1)
    log_a = jax.nn.log_sigmoid((z @ w_gate_up + b_gate).astype(jnp.float32)) / GLA_TAU
    hk = lambda t: t.reshape(B, S, GLA_HEADS, GLA_DK)
    o = gla_chunked(hk(q), hk(k), v.reshape(B, S, GLA_HEADS, GLA_DV), hk(log_a)).astype(xn.dtype)
    o = rms_norm(o, head_gain) * jax.nn.silu(g.reshape(B, S, GLA_HEADS, GLA_DV))
    return o.reshape(B, S, GLA_HEADS * GLA_DV) @ w_out

def shared_kv(h, kv_norm, w_kv, k_norm):
    B, S, _ = h.shape
    kv = rms_norm(h, kv_norm) @ w_kv
    k, v = jnp.split(kv, [DIFF_HEADS * 2 * DIFF_DH], axis=-1)
    k = rms_norm(k.reshape(B, S, DIFF_HEADS, 2, DIFF_DH), k_norm).transpose(0, 2, 3, 1, 4)
    v = v.reshape(B, S, DIFF_HEADS, DIFF_VD).transpose(0, 2, 1, 3)
    return k, v

def diff_mixer(xn, k, v, w_q, q_gain, lam_params, head_gain, w_out, lambda_init):
    B, S, _ = xn.shape
    q = rms_norm((xn @ w_q).reshape(B, S, DIFF_HEADS, 2, DIFF_DH), q_gain) * (DIFF_DH ** -0.5)
    lp = lam_params.astype(jnp.float32)
    lam = jnp.exp(jnp.sum(lp[0] * lp[1])) - jnp.exp(jnp.sum(lp[2] * lp[3])) + lambda_init
    nq = S // Q_BLOCK
    qb = q.transpose(0, 2, 3, 1, 4).reshape(B, DIFF_HEADS, 2, nq, Q_BLOCK, DIFF_DH).transpose(3, 0, 1, 2, 4, 5)
    kpos = jnp.arange(S)

    def attend(args):
        q_blk, bi = args
        s = jnp.einsum('bhcqd,bhckd->bhcqk', q_blk, k).astype(jnp.float32)
        qpos = bi * Q_BLOCK + jnp.arange(Q_BLOCK)
        s = jnp.where(kpos[None, :] <= qpos[:, None], s, -jnp.inf)
        p = jax.nn.softmax(s, axis=-1)
        a = p[:, :, 0] - lam * p[:, :, 1]
        return jnp.einsum('bhqk,bhkv->bhqv', a.astype(v.dtype), v)

    o = lax.map(attend, (qb, jnp.arange(nq)))
    o = o.transpose(1, 0, 3, 2, 4).reshape(B, S, DIFF_HEADS, DIFF_VD)
    o = rms_norm(o, head_gain) * (1.0 - lambda_init)
    return o.reshape(B, S, DIFF_HEADS * DIFF_VD) @ w_out

def first_inputs(seed: int = 0) -> dict:
    key = jax.random.key(seed)
    ks = jax.random.split(key, 24)
    f32 = jnp.float32
    nrm = lambda k, shape, fan_in: jax.random.normal(k, shape, f32) * (fan_in ** -0.5)
    gain = lambda k, shape: 1.0 + 0.02 * jax.random.normal(k, shape, f32)
    D = D_MODEL
    return {
        "x": jax.random.normal(ks[0], (BATCH, SEQ, D), f32),
        "a_norm": gain(ks[1], (N_A, D)),
        "a_w_in": nrm(ks[2], (N_A, D, GLA_IN), D),
        "a_w_gate_up": nrm(ks[3], (N_A, GLA_GATE_RANK, GLA_HEADS * GLA_DK), GLA_GATE_RANK),
        "a_b_gate": 0.1 * jax.random.normal(ks[4], (N_A, GLA_HEADS * GLA_DK), f32),
        "a_head_norm": gain(ks[5], (N_A, GLA_DV)),
        "a_w_out": nrm(ks[6], (N_A, GLA_HEADS * GLA_DV, D), GLA_HEADS * GLA_DV),
        "kv_norm": gain(ks[7], (D,)),
        "w_kv": nrm(ks[8], (D, DIFF_HEADS * (2 * DIFF_DH + DIFF_VD)), D),
        "k_norm": gain(ks[9], (DIFF_DH,)),
        "b_norm": gain(ks[10], (N_B, D)),
        "b_w_q": nrm(ks[11], (N_B, D, DIFF_HEADS * 2 * DIFF_DH), D),
        "b_q_norm": gain(ks[12], (N_B, DIFF_DH)),
        "b_lambda": 0.1 * jax.random.normal(ks[13], (N_B, 4, DIFF_DH), f32),
        "b_head_norm": gain(ks[14], (N_B, DIFF_VD)),
        "b_w_out": nrm(ks[15], (N_B, DIFF_HEADS * DIFF_VD, D), DIFF_HEADS * DIFF_VD),
        "mlp_norm": gain(ks[16], (DEPTH, D)),
        "mlp_w1": nrm(ks[17], (DEPTH, D, MLP_HIDDEN), D),
        "mlp_w2": nrm(ks[18], (DEPTH, MLP_HIDDEN, D), MLP_HIDDEN),
    }

def first_block(x, a_norm, a_w_in, a_w_gate_up, a_b_gate, a_head_norm, a_w_out,
              kv_norm, w_kv, k_norm, b_norm, b_w_q, b_q_norm, b_lambda, b_head_norm, b_w_out,
              mlp_norm, mlp_w1, mlp_w2):
    h = x
    k_sh, v_sh = None, None
    for layer in range(DEPTH):
        if layer < N_A:
            i = layer
            h = h + gla_mixer(rms_norm(h, a_norm[i]), a_w_in[i], a_w_gate_up[i], a_b_gate[i],
                              a_head_norm[i], a_w_out[i])
        else:
            if layer == N_A:
                k_sh, v_sh = shared_kv(h, kv_norm, w_kv, k_norm)
            j = layer - N_A
            lambda_init = 0.8 - 0.6 * math.exp(-0.3 * layer)
            h = h + diff_mixer(rms_norm(h, b_norm[j]), k_sh, v_sh, b_w_q[j], b_q_norm[j],
                               b_lambda[j], b_head_norm[j], b_w_out[j], lambda_init)
        h = h + sqrelu_mlp(rms_norm(h, mlp_norm[layer]), mlp_w1[layer], mlp_w2[layer])
    return h


DEPTH_2 = 1

MEM_LEN = 256
EPS = 1e-6
NEG_INF = -1e30

CONV_DIM = D_MODEL
CONV_KERNEL = 31

SSD_INNER = 2 * D_MODEL
SSD_HEAD_DIM = 64
SSD_HEADS = SSD_INNER // SSD_HEAD_DIM
SSD_GROUPS = 4
SSD_STATE = 128
SSD_CONV = 4
SSD_CHUNK = 128
SSD_XBC = SSD_INNER + 2 * SSD_GROUPS * SSD_STATE

ATTN_HEADS = 16
ATTN_KV_HEADS = 4
ATTN_HEAD_DIM = 64
ATTN_DIM = ATTN_HEADS * ATTN_HEAD_DIM
ATTN_KV_DIM = ATTN_KV_HEADS * ATTN_HEAD_DIM
ATTN_WINDOW = 128
ATTN_BLOCK = 128

REL_BUCKETS = 32
REL_MAX_DIST = 128

XATTN_HEADS = 4
XATTN_HEAD_DIM = D_MODEL // XATTN_HEADS

N_BRANCH = 3
MLP_HIDDEN_2 = 4 * D_MODEL

OFF_CONV = 0
OFF_Z = OFF_CONV + 2 * CONV_DIM
OFF_XBC = OFF_Z + SSD_INNER
OFF_DT = OFF_XBC + SSD_XBC
OFF_Q = OFF_DT + SSD_HEADS
OFF_K = OFF_Q + ATTN_DIM
OFF_V = OFF_K + ATTN_KV_DIM
OFF_GATE = OFF_V + ATTN_KV_DIM
IN_COLS = OFF_GATE + N_BRANCH * D_MODEL


def rms_norm_2(x, g):
    x32 = x.astype(jnp.float32)
    y = x32 * lax.rsqrt(jnp.mean(x32 * x32, axis=-1, keepdims=True) + EPS)
    return (y * g.astype(jnp.float32)).astype(x.dtype)

def layer_norm(x, g, b):
    x32 = x.astype(jnp.float32)
    mu = jnp.mean(x32, axis=-1, keepdims=True)
    xc = x32 - mu
    y = xc * lax.rsqrt(jnp.mean(xc * xc, axis=-1, keepdims=True) + EPS)
    return (y * g.astype(jnp.float32) + b.astype(jnp.float32)).astype(x.dtype)

def causal_depthwise_conv(x, w, b):
    k, c = w.shape
    y = lax.conv_general_dilated(
        x, w[:, None, :].astype(x.dtype), window_strides=(1,), padding=[(k - 1, 0)],
        dimension_numbers=("NWC", "WIO", "NWC"), feature_group_count=c)
    return y + b.astype(x.dtype)

def conformer_conv_branch(u, dw_w, dw_b, ln_g, ln_b):
    a, gate = jnp.split(u, 2, axis=-1)
    h = a * jax.nn.sigmoid(gate)
    h = causal_depthwise_conv(h, dw_w, dw_b)
    h = layer_norm(h, ln_g, ln_b)
    return jax.nn.silu(h)

def segsum_exp(a):
    t = a.shape[-1]
    cs = jnp.cumsum(a, axis=-1)
    diff = cs[..., :, None] - cs[..., None, :]
    mask = jnp.tril(jnp.ones((t, t), dtype=bool))
    return jnp.where(mask, jnp.exp(jnp.where(mask, diff, 0.0)), 0.0)

def ssd_chunked(x, dt, a, bm, cm):
    b, l, h, p = x.shape
    g, n = bm.shape[-2:]
    r = h // g
    q = SSD_CHUNK
    nc = l // q
    xdt = (x * dt[..., None].astype(x.dtype)).reshape(b, nc, q, g, r, p)
    bc = bm.reshape(b, nc, q, g, n)
    cc = cm.reshape(b, nc, q, g, n)
    da = (dt * a).reshape(b, nc, q, g, r).transpose(0, 1, 3, 4, 2)
    cs = jnp.cumsum(da, axis=-1)
    decay = segsum_exp(da).astype(x.dtype)
    cb = jnp.einsum("bcqgn,bcsgn->bcgqs", cc, bc)
    scores = cb[:, :, :, None] * decay
    y_diag = jnp.einsum("bcgrqs,bcsgrp->bcqgrp", scores, xdt)
    decay_to_end = jnp.exp(cs[..., -1:] - cs).astype(x.dtype)
    chunk_states = jnp.einsum("bcqgn,bcgrq,bcqgrp->bcgrpn", bc, decay_to_end, xdt)
    chunk_decay = jnp.exp(cs[..., -1])

    def step(state, inp):
        s_c, d_c = inp
        return state * d_c[..., None, None] + s_c, state

    init = jnp.zeros((b, g, r, p, n), jnp.float32)
    _, states_in = lax.scan(
        step, init,
        (jnp.moveaxis(chunk_states.astype(jnp.float32), 1, 0), jnp.moveaxis(chunk_decay, 1, 0)))
    states_in = jnp.moveaxis(states_in, 0, 1).astype(x.dtype)
    decay_from_start = jnp.exp(cs).astype(x.dtype)
    y_off = jnp.einsum("bcqgn,bcgrpn,bcgrq->bcqgrp", cc, states_in, decay_from_start)
    return (y_diag + y_off).reshape(b, l, h, p)

def ssd_branch(z, xbc, dt_raw, conv_w, conv_b, dt_bias, a_log, d_skip, norm_g):
    b, l, _ = xbc.shape
    xbc = jax.nn.silu(causal_depthwise_conv(xbc, conv_w, conv_b))
    xs = xbc[..., :SSD_INNER].reshape(b, l, SSD_HEADS, SSD_HEAD_DIM)
    bm = xbc[..., SSD_INNER:SSD_INNER + SSD_GROUPS * SSD_STATE].reshape(b, l, SSD_GROUPS, SSD_STATE)
    cm = xbc[..., SSD_INNER + SSD_GROUPS * SSD_STATE:].reshape(b, l, SSD_GROUPS, SSD_STATE)
    dt = jax.nn.softplus(dt_raw.astype(jnp.float32) + dt_bias.astype(jnp.float32))
    a = -jnp.exp(a_log.astype(jnp.float32))
    y = ssd_chunked(xs, dt, a, bm, cm) + xs * d_skip[:, None].astype(xs.dtype)
    y = y.reshape(b, l, SSD_INNER) * jax.nn.silu(z)
    y = rms_norm_2(y.reshape(b, l, SSD_GROUPS, SSD_INNER // SSD_GROUPS),
                 norm_g.reshape(SSD_GROUPS, SSD_INNER // SSD_GROUPS))
    return y.reshape(b, l, SSD_INNER)

def t5_band_bias(rel_table):
    qi = jnp.arange(ATTN_BLOCK)[:, None] + ATTN_BLOCK
    kj = jnp.arange(2 * ATTN_BLOCK)[None, :]
    dist = qi - kj
    max_exact = REL_BUCKETS // 2
    d = jnp.maximum(dist, 1).astype(jnp.float32)
    large = max_exact + (jnp.log(d / max_exact) / math.log(REL_MAX_DIST / max_exact)
                         * (REL_BUCKETS - max_exact)).astype(jnp.int32)
    large = jnp.minimum(large, REL_BUCKETS - 1)
    bucket = jnp.where(dist < max_exact, jnp.maximum(dist, 0), large)
    bias = jnp.transpose(rel_table[bucket], (2, 0, 1)).astype(jnp.float32)
    return bias, dist

def swa_branch(q, k, v, q_g, k_g, sinks, rel_bias, band_dist):
    b, l, _ = q.shape
    nb = l // ATTN_BLOCK
    r = ATTN_HEADS // ATTN_KV_HEADS
    q = rms_norm_2(q.reshape(b, l, ATTN_HEADS, ATTN_HEAD_DIM), q_g)
    k = rms_norm_2(k.reshape(b, l, ATTN_KV_HEADS, ATTN_HEAD_DIM), k_g)
    v = v.reshape(b, l, ATTN_KV_HEADS, ATTN_HEAD_DIM)

    def band(t):
        tp = jnp.pad(t, ((0, 0), (ATTN_BLOCK, 0), (0, 0), (0, 0)))
        prev = tp[:, :l].reshape(b, nb, ATTN_BLOCK, ATTN_KV_HEADS, ATTN_HEAD_DIM)
        cur = t.reshape(b, nb, ATTN_BLOCK, ATTN_KV_HEADS, ATTN_HEAD_DIM)
        return jnp.concatenate([prev, cur], axis=2)

    kb, vb = band(k), band(v)
    qb = q.reshape(b, nb, ATTN_BLOCK, ATTN_KV_HEADS, r, ATTN_HEAD_DIM)
    logits = jnp.einsum("bnqgrd,bnkgd->bngrqk", qb, kb).astype(jnp.float32) * (ATTN_HEAD_DIM ** -0.5)
    logits = logits + rel_bias.reshape(ATTN_KV_HEADS, r, ATTN_BLOCK, 2 * ATTN_BLOCK)
    key_pos = (jnp.arange(nb)[:, None] * ATTN_BLOCK - ATTN_BLOCK
               + jnp.arange(2 * ATTN_BLOCK)[None, :])
    in_window = (band_dist >= 0) & (band_dist < ATTN_WINDOW)
    mask = in_window[None] & (key_pos >= 0)[:, None, :]
    logits = jnp.where(mask[None, :, None, None], logits, NEG_INF)
    sink = sinks.astype(jnp.float32).reshape(ATTN_KV_HEADS, r)[None, None, :, :, None, None]
    m = jnp.maximum(jnp.max(logits, axis=-1, keepdims=True), sink)
    pexp = jnp.exp(logits - m)
    probs = pexp / (jnp.sum(pexp, axis=-1, keepdims=True) + jnp.exp(sink - m))
    out = jnp.einsum("bngrqk,bnkgd->bnqgrd", probs.astype(v.dtype), vb)
    return out.reshape(b, l, ATTN_DIM)

def memory_cross_attention(h, mem_h, w_q, w_kv, q_g, k_g, w_o):
    b, l, _ = h.shape
    m = mem_h.shape[1]
    q = rms_norm_2((h @ w_q).reshape(b, l, XATTN_HEADS, XATTN_HEAD_DIM), q_g)
    kv = mem_h @ w_kv
    k = rms_norm_2(kv[..., :D_MODEL].reshape(b, m, XATTN_HEADS, XATTN_HEAD_DIM), k_g)
    v = kv[..., D_MODEL:].reshape(b, m, XATTN_HEADS, XATTN_HEAD_DIM)
    logits = jnp.einsum("bqhd,bkhd->bhqk", q, k).astype(jnp.float32) * (XATTN_HEAD_DIM ** -0.5)
    probs = jax.nn.softmax(logits, axis=-1)
    out = jnp.einsum("bhqk,bkhd->bqhd", probs.astype(v.dtype), v).reshape(b, l, D_MODEL)
    return out @ w_o

def second_inputs(seed: int = 0) -> dict:
    key = jax.random.key(seed)
    ks = iter(jax.random.split(key, 48))
    f32 = jnp.float32
    L = DEPTH_2

    def nrm(shape, scale):
        return jax.random.normal(next(ks), shape, f32) * scale

    def gain(shape):
        return 1.0 + nrm(shape, 0.02)

    out_scale = (2.0 * DEPTH_2) ** -0.5
    dt0 = jnp.exp(jax.random.uniform(next(ks), (L, SSD_HEADS), f32, math.log(1e-3), math.log(1e-1)))
    return {
        "x": nrm((BATCH, SEQ, D_MODEL), 1.0),
        "mem": nrm((BATCH, MEM_LEN, D_MODEL), 1.0),
        "rel_table": nrm((REL_BUCKETS, ATTN_HEADS), 0.1),
        "norm_mix": gain((L, D_MODEL)),
        "w_in": nrm((L, D_MODEL, IN_COLS), D_MODEL ** -0.5),
        "gate_bias": nrm((L, N_BRANCH, D_MODEL), 0.01),
        "conv_dw_w": nrm((L, CONV_KERNEL, CONV_DIM), CONV_KERNEL ** -0.5),
        "conv_dw_b": nrm((L, CONV_DIM), 0.01),
        "conv_ln_g": gain((L, CONV_DIM)),
        "conv_ln_b": nrm((L, CONV_DIM), 0.01),
        "w_conv_out": nrm((L, CONV_DIM, D_MODEL), CONV_DIM ** -0.5),
        "ssd_conv_w": nrm((L, SSD_CONV, SSD_XBC), SSD_CONV ** -0.5),
        "ssd_conv_b": nrm((L, SSD_XBC), 0.01),
        "ssd_dt_bias": dt0 + jnp.log(-jnp.expm1(-dt0)),
        "ssd_A_log": jnp.log(jax.random.uniform(next(ks), (L, SSD_HEADS), f32, 1.0, 16.0)),
        "ssd_D": gain((L, SSD_HEADS)),
        "ssd_norm_g": gain((L, SSD_INNER)),
        "w_ssd_out": nrm((L, SSD_INNER, D_MODEL), SSD_INNER ** -0.5),
        "attn_q_norm": gain((L, ATTN_HEAD_DIM)),
        "attn_k_norm": gain((L, ATTN_HEAD_DIM)),
        "attn_sinks": nrm((L, ATTN_HEADS), 0.5),
        "w_attn_out": nrm((L, ATTN_DIM, D_MODEL), ATTN_DIM ** -0.5),
        "w_mix_out": nrm((L, D_MODEL, D_MODEL), out_scale * D_MODEL ** -0.5),
        "norm_xattn": gain((L, D_MODEL)),
        "norm_mem": gain((L, D_MODEL)),
        "w_xq": nrm((L, D_MODEL, D_MODEL), D_MODEL ** -0.5),
        "w_xkv": nrm((L, D_MODEL, 2 * D_MODEL), D_MODEL ** -0.5),
        "xattn_q_norm": gain((L, XATTN_HEAD_DIM)),
        "xattn_k_norm": gain((L, XATTN_HEAD_DIM)),
        "w_xo": nrm((L, D_MODEL, D_MODEL), out_scale * D_MODEL ** -0.5),
        "norm_mlp": gain((L, D_MODEL)),
        "w_mlp_up": nrm((L, D_MODEL, MLP_HIDDEN_2), D_MODEL ** -0.5),
        "w_mlp_down": nrm((L, MLP_HIDDEN_2, D_MODEL), out_scale * MLP_HIDDEN_2 ** -0.5),
    }

def second_block(x, mem, rel_table, norm_mix, w_in, gate_bias, conv_dw_w, conv_dw_b, conv_ln_g,
              conv_ln_b, w_conv_out, ssd_conv_w, ssd_conv_b, ssd_dt_bias, ssd_A_log, ssd_D,
              ssd_norm_g, w_ssd_out, attn_q_norm, attn_k_norm, attn_sinks, w_attn_out, w_mix_out,
              norm_xattn, norm_mem, w_xq, w_xkv, xattn_q_norm, xattn_k_norm, w_xo, norm_mlp,
              w_mlp_up, w_mlp_down):
    b, l, _ = x.shape
    rel_bias, band_dist = t5_band_bias(rel_table)
    h = x
    for i in range(DEPTH_2):
        u = rms_norm_2(h, norm_mix[i])
        proj = u @ w_in[i]
        y_a = conformer_conv_branch(proj[..., OFF_CONV:OFF_Z], conv_dw_w[i], conv_dw_b[i],
                                    conv_ln_g[i], conv_ln_b[i]) @ w_conv_out[i]
        y_b = ssd_branch(proj[..., OFF_Z:OFF_XBC], proj[..., OFF_XBC:OFF_DT], proj[..., OFF_DT:OFF_Q],
                         ssd_conv_w[i], ssd_conv_b[i], ssd_dt_bias[i], ssd_A_log[i], ssd_D[i],
                         ssd_norm_g[i]) @ w_ssd_out[i]
        y_c = swa_branch(proj[..., OFF_Q:OFF_K], proj[..., OFF_K:OFF_V], proj[..., OFF_V:OFF_GATE],
                         attn_q_norm[i], attn_k_norm[i], attn_sinks[i], rel_bias, band_dist) @ w_attn_out[i]
        gates = jax.nn.sigmoid(proj[..., OFF_GATE:IN_COLS].reshape(b, l, N_BRANCH, D_MODEL)
                               + gate_bias[i].astype(proj.dtype))
        merged = gates[..., 0, :] * y_a + gates[..., 1, :] * y_b + gates[..., 2, :] * y_c
        h = h + merged @ w_mix_out[i]
        h = h + memory_cross_attention(rms_norm_2(h, norm_xattn[i]), rms_norm_2(mem, norm_mem[i]),
                                       w_xq[i], w_xkv[i], xattn_q_norm[i], xattn_k_norm[i], w_xo[i])
        u = rms_norm_2(h, norm_mlp[i])
        h = h + jnp.square(jax.nn.relu(u @ w_mlp_up[i])) @ w_mlp_down[i]
    return h


def setup_inputs(seed=0):
    out = dict(first_inputs(seed))
    for name, value in second_inputs(seed + 1).items():
        if name != "x":
            out[name + "_2"] = value
    return out


def reference(
    x, a_norm, a_w_in, a_w_gate_up, a_b_gate, a_head_norm, a_w_out, kv_norm, w_kv, k_norm,
    b_norm, b_w_q, b_q_norm, b_lambda, b_head_norm, b_w_out, mlp_norm, mlp_w1, mlp_w2, mem_2,
    rel_table_2, norm_mix_2, w_in_2, gate_bias_2, conv_dw_w_2, conv_dw_b_2, conv_ln_g_2,
    conv_ln_b_2, w_conv_out_2, ssd_conv_w_2, ssd_conv_b_2, ssd_dt_bias_2, ssd_A_log_2, ssd_D_2,
    ssd_norm_g_2, w_ssd_out_2, attn_q_norm_2, attn_k_norm_2, attn_sinks_2, w_attn_out_2,
    w_mix_out_2, norm_xattn_2, norm_mem_2, w_xq_2, w_xkv_2, xattn_q_norm_2, xattn_k_norm_2,
    w_xo_2, norm_mlp_2, w_mlp_up_2, w_mlp_down_2,
):
    x = first_block(
        x, a_norm, a_w_in, a_w_gate_up, a_b_gate, a_head_norm, a_w_out, kv_norm, w_kv, k_norm,
        b_norm, b_w_q, b_q_norm, b_lambda, b_head_norm, b_w_out, mlp_norm, mlp_w1, mlp_w2,
    )
    return second_block(
        x, mem_2, rel_table_2, norm_mix_2, w_in_2, gate_bias_2, conv_dw_w_2, conv_dw_b_2,
        conv_ln_g_2, conv_ln_b_2, w_conv_out_2, ssd_conv_w_2, ssd_conv_b_2, ssd_dt_bias_2,
        ssd_A_log_2, ssd_D_2, ssd_norm_g_2, w_ssd_out_2, attn_q_norm_2, attn_k_norm_2,
        attn_sinks_2, w_attn_out_2, w_mix_out_2, norm_xattn_2, norm_mem_2, w_xq_2, w_xkv_2,
        xattn_q_norm_2, xattn_k_norm_2, w_xo_2, norm_mlp_2, w_mlp_up_2, w_mlp_down_2,
    )


_drawn_inputs = setup_inputs


def setup_inputs(seed=0):
    import zlib

    import numpy as np

    out = dict(_drawn_inputs(seed))
    spreads = {}
    factors = {'a_head_norm': 4.422,
     'kv_norm': 6.182,
     'k_norm': 8.0,
     'b_norm': 8.0,
     'b_q_norm': 8.0,
     'b_lambda': 8.0,
     'b_head_norm': 7.392,
     'rel_table_2': 8.0,
     'norm_mix_2': 8.0,
     'gate_bias_2': 8.0,
     'conv_dw_b_2': 8.0,
     'conv_ln_g_2': 8.0,
     'conv_ln_b_2': 25.029,
     'ssd_conv_b_2': 8.0,
     'ssd_D_2': 64.0,
     'ssd_norm_g_2': 8.0,
     'attn_q_norm_2': 8.0,
     'attn_k_norm_2': 8.0,
     'attn_sinks_2': 33.061,
     'norm_xattn_2': 8.0,
     'norm_mem_2': 8.0,
     'xattn_q_norm_2': 8.0,
     'xattn_k_norm_2': 8.0,
     'norm_mlp_2': 6.603}
    for name, (base, spread) in spreads.items():
        noise = np.random.default_rng([zlib.crc32(name.encode()), seed]).standard_normal(out[name].shape)
        drawn = base * np.exp(spread * noise) if base else spread * noise
        out[name] = __import__('jax').numpy.asarray(drawn.astype(out[name].dtype))
    for name, factor in factors.items():
        out[name] = (out[name] * factor).astype(out[name].dtype)
    return out
```

```python
from contextlib import ExitStack

import numpy as np
import concourse.bass as bass
from concourse import mybir

F32 = mybir.dt.float32
F32R = mybir.dt.float32r
BF16 = mybir.dt.bfloat16
ALU = mybir.AluOpType
ACT = mybir.ActivationFunctionType
AX = mybir.AxisListType

P = 128
D = 1024
T = 256
KC = D // P
NT = T // P
EPS = 1e-6
NEG = -1e30

GLA_HEADS, GLA_RANK, GLA_TAU = 4, 16, 16.0
DIFF_HEADS, DIFF_DH = 8, 64
LAMBDA_INIT = 0.8 - 0.6 * float(np.exp(-0.3))
TAPS, SSD_TAPS = 31, 4
SSD_HEADS, SSD_GROUPS = 32, 4
SWA_HEADS, SWA_KV, SWA_DH = 16, 4, 64
SWA_PAIRS = SWA_HEADS // 2
X_HEADS = 4
HID_GROUPS = 4
BAND = 3 * P

C_QK, C_GV, C_GG, C_GO, C_M0 = 0, 8, 16, 24, 32
C_DK, C_DV, C_DQ, C_DO, C_M1 = 96, 104, 112, 120, 128
C_CONV, C_XBC, C_Z, C_YA, C_YB0, C_YB1, C_SWA, C_YC, C_MIX = 192, 208, 232, 248, 264, 280, 288, 300, 316
C_XK, C_XV, C_XQ, C_XO, C_M2 = 324, 332, 340, 348, 356
CHUNKS = 420
SLABS = CHUNKS // 2
RING = 4
AHEAD = 3
HI_SLOTS = 4
BANKS = 4
DIFF_BANKS = (2, 4)
SWA_BANKS = (1, 4)
OUT_BANKS = (7, 3)

PARAMS = [
    ("a_norm", 8), ("a_head_norm", 2), ("kv_norm", 8), ("b_norm", 8), ("mlp_norm0", 8), ("mlp_norm1", 8),
    ("k_norm", 1), ("b_q_norm", 1), ("b_head_norm", 1), ("norm_mix", 8), ("conv_b", 8), ("ln_g", 8), ("ln_b", 8),
    ("conv_w", KC * TAPS), ("ssd_conv_b", 24), ("ssd_conv_w", 24 * SSD_TAPS), ("ssd_D", 16), ("ssd_norm", 16),
    ("gate_bias", 24), ("swa_q_norm", 1), ("swa_k_norm", 1), ("norm_xattn", 8), ("norm_mem", 8),
    ("xq_norm", 2), ("xk_norm", 2), ("norm_mlp2", 8), ("dt_bias", SSD_HEADS), ("A_log", SSD_HEADS),
    ("sinks", SWA_HEADS), ("b_lambda", 4 * DIFF_DH), ("w_z", KC * GLA_RANK), ("w_dt", KC * SSD_HEADS),
    ("gate_up", 512), ("rel", SWA_HEADS),
]
PCOL, NPAR = {}, 0
for _name, _width in PARAMS:
    PCOL[_name] = NPAR
    NPAR += _width
CONSTS = [("ident", P), ("bones", P), ("upto", P), ("after", P), ("oh", BAND)]
CCOL, NCON = {}, 0
for _name, _width in CONSTS:
    CCOL[_name] = NCON
    NCON += _width
LEVELS = 7
GLA_MASKS = (LEVELS + 2) * P + (LEVELS + 1) * P


def program(nc, w_d, par_d, con_d, gm_d, x_d, mem_d, band_d, out_d):
    ctx = ExitStack()
    with ctx:
        def sb(name, shape, dt=F32):
            return ctx.enter_context(nc.sbuf_tensor(name, shape, dt))

        def sem(name):
            return ctx.enter_context(nc.semaphore(name))

        raw = sb("raw", [P, RING, 2, D])
        w_hi = sb("w_hi", [P, HI_SLOTS, KC, P], F32R)
        w_lo = sb("w_lo", [P, HI_SLOTS, KC, P], BF16)
        H = sb("H", [P, KC, T])
        par = sb("par", [P, NPAR])
        con = sb("con", [P, NCON])
        ones = sb("ones", [P, P])
        ident_b = sb("ident_b", [P, P], BF16)
        later_b = sb("later_b", [P, P], BF16)
        eps = sb("eps", [P, 1])
        one = sb("one", [P, 1])
        sumsq = sb("sumsq", [P, T])
        sqtmp = sb("sqtmp", [P, T])
        lnt = sb("lnt", [P, 2, T])
        lnt_tok = sb("lnt_tok", [P, NT])
        rstd = sb("rstd", [P, T])
        rstd_mem = sb("rstd_mem", [P, T])
        rtok = sb("rtok", [P, NT])
        rtok_mem = sb("rtok_mem", [P, NT])
        hn_sqb = sb("hn_sqb", [P, 2, T])
        hn_rb = sb("hn_rb", [P, 2, T])
        gains = sb("gains", [P, 8])
        ARENA = 20480
        arena = sb("arena", [P, ARENA])
        ps = ctx.enter_context(nc.psum_tensor("ps", [P, 8, 512], F32))

        class XSet:

            def __init__(self, name):
                self.hi = sb(name + "_hi", [P, KC, T], F32R)
                self.lo = sb(name + "_lo", [P, KC, T], F32R)
                self.bf = sb(name + "_bf", [P, KC, T], BF16)
                self.hi_done, self.lo_done, self.bf_done = sem(name + "_hi_done"), sem(name + "_lo_done"), sem(name + "_bf_done")

        XA, XB = XSet("xa"), XSet("xb")

        def pcol(name, i=0, n=1):
            return par[:, PCOL[name] + i:PCOL[name] + i + n]

        def ccol(name, rows=P, n=P):
            return con[0:rows, CCOL[name]:CCOL[name] + n]

        ident, bones, upto_m, after_m = ccol("ident"), ccol("bones"), ccol("upto"), ccol("after")

        class Cut:

            def __init__(self, at=0):
                self.at = at

            def __call__(self, *shape, rows=P):
                n = int(np.prod(shape))
                a = arena[0:rows, self.at:self.at + n]
                self.at += n
                assert self.at <= ARENA, self.at
                if len(shape) == 2:
                    return a.rearrange("p (a b) -> p a b", a=shape[0])
                if len(shape) == 3:
                    return a.rearrange("p (a b c) -> p a b c", a=shape[0], b=shape[1])
                return a

        cut = Cut()
        g_masks = cut(GLA_MASKS)
        g_ranges = g_masks[:, 0:(LEVELS + 2) * P]
        g_pairs = g_masks[:, (LEVELS + 2) * P:]
        g_q, g_k = cut(GLA_HEADS, T), cut(GLA_HEADS, T)
        g_v = cut(NT, D)
        g_gate = cut(KC, T)
        g_la = cut(NT, 512)
        g_lt = cut(NT, 512)
        decayed_at = cut.at
        g_ke = cut(2, (LEVELS + 1) * P)
        g_qe = cut(2, (LEVELS + 1) * P)
        g_kx, g_qx = cut(GLA_HEADS, P), cut(GLA_HEADS, P)
        g_sm = cut((LEVELS + 1) * P)
        g_att = cut(GLA_HEADS, 3, P)
        g_z = cut(T, rows=GLA_RANK + 1 + 15)
        cut = Cut(decayed_at)
        g_sq = cut(2, 2, T)
        g_ro = cut(2, T)
        g_on = cut(2, 2, T)
        cut = Cut()
        m_relu, m_sq = cut(2, T), cut(2, T)
        cut = Cut(1024)
        d_k, d_q = cut(DIFF_HEADS, T), cut(DIFF_HEADS, T)
        d_v = cut(NT, D)
        d_p = cut(2, 2, T)
        d_a0 = cut(2, T)
        d_a = cut(2, T)
        d_at = cut(2, T)
        d_sq, d_ro, d_on = cut(2, T), cut(2, T), cut(2, T)
        d_st = cut(2, 8)
        d_lam = cut(8)
        d_lp = cut(2, DIFF_DH)
        w_row = cut(2, BAND)
        cut = Cut(0)
        s_small = cut(12, NT * SSD_HEADS)
        merged = cut(KC, T)
        s_xbc = cut(24, T)
        s_z = cut(16, T)
        gate_b = s_z[:, 0:KC]
        branch_at = cut.at
        PADW = TAPS - 1 + T
        c_in = cut(KC, PADW)
        c_out = cut(KC, T)
        s_pad = cut(2, SSD_TAPS - 1 + T)
        s_tap = cut(2, T)
        c_tmp = cut(2, T)
        y_gate = arena[:, branch_at + KC * (PADW + T):branch_at + KC * (PADW + T) + 2 * T].rearrange("p (a b) -> p a b", a=2)
        cut = Cut(branch_at)
        s_xd = cut(2, NT, 512)
        s_xd2 = cut(2, 512)
        s_cb = cut(3, P)
        s_e = cut(2, 4 * P)
        s_sc = cut(2, 4 * P)
        s_eb = cut(2, P)
        s_off = cut(2, P)
        s_sq = cut(2, T)
        s_rg = cut(T)
        y_tmp = cut(2, T)
        cut = Cut(768 + 2048)
        w_q, w_k2, w_kd = cut(8, T), cut(2, T), cut(SWA_KV, T)
        w_v = cut(NT, 256)
        w_bias = cut(2, 2, T)
        w_s = cut(2, 2, T)
        w_p = cut(2, 2, T)
        w_pt = cut(2, 2, T)
        w_st = cut(2, 16)
        assert cut.at <= branch_at
        x_mem = Cut(branch_at)(KC, T)
        cut = Cut(768 + 2048)
        x_k, x_q = cut(KC, T), cut(KC, T)
        x_v = cut(NT, D)
        x_sq, x_rk = cut(2, 2, T), cut(2, T)
        x_p = cut(2, 2, T)
        x_pt = cut(2, 2, T)
        x_st = cut(2, 8)
        assert cut.at <= branch_at

        slab_in = [sem(f"slab_in{i}") for i in range(RING)]
        hi_done = sem("hi_done")
        lo_done = sem("lo_done")
        gemm_done = sem("gemm_done")
        bank_free = sem("bank_free")
        in_done, par_done, con_done, mask_done, mem_in = [sem(n) for n in ("in_done", "par_done", "con_done", "mask_done", "mem_in")]
        set_done, bf_set, pad_set = sem("set_done"), sem("bf_set"), sem("pad_set")
        sq_step = sem("sq_step")
        stat_mm, ln_done, rstd_done = sem("stat_mm"), sem("ln_done"), sem("rstd_done")
        sq_done = sem("sq_done")
        hn_sq, hn_mm, hn_ln, hn_r, hn_out = [sem("hn_" + n) for n in ("sq", "mm", "ln", "r", "out")]
        out_done = sem("out_done")
        band_set, band_mm, band_out, band_in = sem("band_set"), sem("band_mm"), [sem("band_out0"), sem("band_out1")], [sem("band_in0"), sem("band_in1")]
        dve_step = sem("dve_step")
        act_step = sem("act_step")
        ga = {n: sem("g_" + n) for n in ("z", "zs", "logit", "abs", "sp", "la", "d", "e", "qk", "s", "m", "silu",
                                         "o", "sq", "n", "r", "on")}
        da = {n: sem("d_" + n) for n in ("s", "max", "p", "a", "t", "at", "o", "sq", "n", "r", "on", "lam", "lame")}
        ca = {n: sem("c_" + n) for n in ("sig", "in", "tap", "mean", "xc", "sq", "var", "r", "norm", "silu")}
        sa = {n: sem("s_" + n) for n in ("tap", "silu", "z", "dt", "dtx", "dta", "dte", "da", "cs", "bias", "x", "xd", "cb", "cbs", "c", "e",
                                         "sc", "y", "yd", "sq", "n", "r", "on", "eb")}
        merged_done = sem("merged_done")
        gate_done = sem("gate_done")
        wa = {n: sem("w_" + n) for n in ("dup", "kd", "s", "ss", "max", "m", "p", "r", "t", "pt", "o")}
        xa = {n: sem("x_" + n) for n in ("sq", "mm", "r", "out", "s", "max", "p", "n", "t", "pt", "o")}

        block = ctx.enter_context(nc.Block())


        def stat_rstd():
            return ps[:, 6, 0:T]

        def stat_tok():
            return ps[:, 6, T:T + NT]

        def diff_scores_at(u):
            return ps[:, DIFF_BANKS[u % 2]:DIFF_BANKS[u % 2] + 2, :]

        def swa_scores_at(u):
            return ps[:, SWA_BANKS[u % 2]:SWA_BANKS[u % 2] + 2, :]

        @block.sync
        def _(sp):
            sp.dma_start(H[:], x_d).then_inc(in_done, 16)
            sp.dma_start(par[:], par_d).then_inc(par_done, 16)
            sp.dma_start(con[:], con_d).then_inc(con_done, 16)
            for s in range(RING):
                sp.dma_start(raw[:, s].rearrange("p a b -> p (a b)"), w_d[s]).then_inc(slab_in[s], 16)
                if s == 1:
                    sp.dma_start(g_masks, gm_d).then_inc(mask_done, 16)

            def slab(s, i):
                sp.wait_ge(hi_done, 2 * (s - RING) + 2)
                sp.wait_ge(lo_done, 2 * (s - RING) + 2)
                sp.dma_start(raw[:, i].rearrange("p a b -> p (a b)"),
                             w_d[bass.ds(s, 1)].rearrange("o p a -> p (o a)")).then_inc(slab_in[i], 16)

            with sp.Fori(1, SLABS // RING) as r:
                for i in range(RING):
                    slab(RING * r + i, i)
            for s in range(SLABS // RING * RING, SLABS):
                slab(s, s % RING)

        @block.tensor
        def _(pe):
            mm = nc.tensor.matmul

            def chunk(c, j, X, build, token_major=False):
                s, bank = j % HI_SLOTS, j % BANKS
                pe.wait_ge(hi_done, c + 1)
                pe.wait_ge(lo_done, c + 1)
                if not isinstance(c, int) or c >= BANKS:
                    pe.wait_ge(bank_free, c - BANKS + 1)
                if not token_major:
                    for k in range(KC):
                        if build is not None:
                            pe.wait_ge(X.bf_done, KC * build + k + 1)
                            pe.wait_ge(X.lo_done, KC * build + k + 1)
                        mm(ps[:, bank, 0:T], w_hi[:, s, k], X.hi[:, k], start=k == 0, stop=False)
                        mm(ps[:, bank, 0:T], w_hi[:, s, k], X.lo[:, k], start=False, stop=False)
                        last = mm(ps[:, bank, 0:T], w_lo[:, s, k], X.bf[:, k], start=False, stop=k == KC - 1)
                else:
                    if build is not None:
                        pe.wait_ge(X.bf_done, KC * build + KC)
                        pe.wait_ge(X.lo_done, KC * build + KC)
                    for t in range(NT):
                        at = slice(t * P, (t + 1) * P)
                        for k in range(KC):
                            mm(ps[:, bank, at], X.hi[:, k, at], w_hi[:, s, k], start=k == 0, stop=False)
                            mm(ps[:, bank, at], X.lo[:, k, at], w_hi[:, s, k], start=False, stop=False)
                            last = mm(ps[:, bank, at], X.bf[:, k, at], w_lo[:, s, k], start=False, stop=k == KC - 1)
                last.then_inc(gemm_done, 1)

            def chunks(c0, n, X, build, token_major=False):
                for j in range(n):
                    chunk(c0 + j, c0 + j, X, build if j == 0 else None, token_major)

            def stats(nu, tok):
                pe.wait_ge(sq_step, (2 * KC - 1) * (nu + 1))
                if nu:
                    pe.wait_ge(rstd_done, nu)
                last = mm(stat_rstd(), ones[:], sumsq[:], start=True, stop=True)
                if tok:
                    for t in range(NT):
                        last = mm(stat_tok()[:, t:t + 1], sumsq[:, t * P:(t + 1) * P], ones[:, 0:1], start=True, stop=True)
                last.then_inc(stat_mm, 1)

            def head_sums(k):
                pe.wait_ge(hn_sq, k + 1)
                if k >= 2:
                    pe.wait_ge(hn_ln, k - 1)
                mm(ps[:, 4 + k % 2, 0:T], bones, hn_sqb[:, k % 2], start=True, stop=True).then_inc(hn_mm, 1)

            def mlp(c0, x_build, xb_build0, nu):
                def group(g, first):
                    c = c0 + 16 * g
                    o = c0 % 8
                    for j in range(8):
                        chunk(c + j, o + j, XA, x_build if first and j == 0 else None)
                        if first and j == 0:
                            stats(nu, False)
                    for j in range(8):
                        chunk(c + 8 + j, o + j, XB, xb_build0 + g if j == 0 else None)
                group(0, True)
                with pe.Fori(1, HID_GROUPS) as g:
                    group(g, False)

            pe.wait_ge(set_done, 1)
            chunk(0, 0, XA, 0)
            stats(0, True)
            chunks(1, 3, XA, None)
            wz = par[:, PCOL["w_z"]:PCOL["w_z"] + KC * GLA_RANK].rearrange("p (k r) -> p k r", k=KC)
            for k in range(KC):
                mm(ps[0:GLA_RANK, 7, 0:T], wz[:, k], XA.hi[:, k].bitcast(F32), start=k == 0, stop=False)
                last = mm(ps[0:GLA_RANK, 7, 0:T], wz[:, k], XA.lo[:, k].bitcast(F32), start=False, stop=k == KC - 1)
            last.then_inc(ga["z"], 1)
            chunks(4, 2, XA, None)
            pe.wait_ge(ga["zs"], 2)
            n = GLA_RANK + 1
            for t in range(NT):
                mm(ps[:, 4 + t, :], g_z[0:n, t * P:(t + 1) * P], par[0:n, PCOL["gate_up"]:PCOL["gate_up"] + 512],
                   start=True, stop=True).then_inc(ga["logit"], 1)
            chunks(6, 2, XA, None)

            def decays(u):
                h, t = u // 2, u % 2
                if u == 0:
                    pe.wait_ge(mask_done, 16)
                    pe.wait_ge(ga["la"], NT)
                else:
                    pe.wait_ge(ga["e"], u)
                for b in range(2):
                    last = mm(ps[:, 4 + b, :], g_la[:, t, h * P:(h + 1) * P],
                              g_ranges[:, t * P + b * 512:t * P + (b + 1) * 512], start=True, stop=True)
                last.then_inc(ga["d"], 1)

            def scores(u):
                h, t = u // 2, u % 2
                pe.wait_ge(ga["qk"], u + 1)
                if u:
                    pe.wait_ge(ga["m"], u)
                skip = 1 - t
                at = slice(t * P, (t + 1) * P)
                for lv in range(LEVELS):
                    lo = (lv + skip) * P
                    mm(ps[:, 6 + lv // 4, lv % 4 * P:(lv % 4 + 1) * P], g_ke[:, u % 2, lo:lo + P], g_qe[:, u % 2, lo:lo + P],
                       start=True, stop=True)
                last = mm(ps[:, 7, 3 * P:4 * P], g_k[:, h, at], g_q[:, h, at], start=True, stop=True)
                last.then_inc(ga["s"], 1)

            for u in range(2 * GLA_HEADS + 1):
                if u < 2 * GLA_HEADS:
                    for c in (8 + 2 * u, 9 + 2 * u):
                        chunk(c, c, XA, None, token_major=c < C_GG)
                    decays(u)
                if u:
                    scores(u - 1)
            pe.wait_ge(ga["e"], 2 * GLA_HEADS)
            for h in range(GLA_HEADS):
                last = mm(ps[:, 4, h * P:(h + 1) * P], g_kx[:, h], g_qx[:, h], start=True, stop=True)
            last.then_inc(ga["s"], 1)
            for h in range(GLA_HEADS + 1):
                if h < GLA_HEADS:
                    b = 4 + h % 2
                    pe.wait_ge(ga["m"], 2 * GLA_HEADS + 1)
                    pe.wait_ge(bank_free, C_GG)
                    if h >= 2:
                        pe.wait_ge(ga["on"], 2 * (h - 1))
                    for half in range(2):
                        f = slice(h * T + half * P, h * T + (half + 1) * P)
                        o = ps[:, b, half * T:(half + 1) * T]
                        mm(o[:, 0:P], g_v[:, 0, f], g_att[:, h, 0], start=True, stop=True)
                        mm(o[:, P:T], g_v[:, 0, f], g_att[:, h, 2], start=True, stop=False)
                        last = mm(o[:, P:T], g_v[:, 1, f], g_att[:, h, 1], start=False, stop=True)
                    last.then_inc(ga["o"], 1)
                if h:
                    pe.wait_ge(ga["sq"], h)
                    if h >= 3:
                        pe.wait_ge(ga["r"], h - 2)
                    mm(ps[:, 6 + (h - 1) % 2, 0:T], ones[:], g_sq[:, (h - 1) % 2, 0], start=True, stop=False)
                    mm(ps[:, 6 + (h - 1) % 2, 0:T], ones[:], g_sq[:, (h - 1) % 2, 1], start=False, stop=True).then_inc(ga["n"], 1)

            chunks(C_GO, 8, XB, 0)
            mlp(C_M0, 1, 1, 1)

            for n in range(9):
                if n < 8:
                    chunk(C_DK + n, n, XA, 2 if n == 0 else None)
                    if n == 0:
                        stats(2, True)
                if n:
                    head_sums(n - 1)
            for h in range(SWA_HEADS):
                if h % 2 == 0:
                    chunk(C_DV + h // 2, h // 2, XA, None, token_major=True)
                if h >= 2:
                    pe.wait_ge(band_set, h - 1)
                mm(ps[:, 6 + h % 2, 0:BAND], par[0:33, PCOL["rel"] + h:PCOL["rel"] + h + 1].to_broadcast([33, P]),
                   con[0:33, CCOL["oh"]:CCOL["oh"] + BAND], start=True, stop=True).then_inc(band_mm, 1)
            for n in range(9):
                if n < 8:
                    chunk(C_DQ + n, n, XB, 5 if n == 0 else None)
                if n:
                    head_sums(8 + n - 1)

            def diff_scores(u):
                h, t = u // 2, u % 2
                if u >= 2:
                    pe.wait_ge(da["p"], u - 1)
                s = diff_scores_at(u)
                for c in range(2):
                    rows = slice(64 * c, 64 * c + 64)
                    mm(s[:, c, 0:(t + 1) * P], d_q[rows, h, t * P:(t + 1) * P], d_k[rows, h, 0:(t + 1) * P],
                       start=True, stop=False)
                    last = mm(s[:, c, t * P:(t + 1) * P], ident_b[:], later_b[:], start=False, stop=True)
                last.then_inc(da["s"], 1)

            pe.wait_ge(hn_out, 16)
            pe.wait_ge(bf_set, 2)
            diff_scores(0)
            for u in range(2 * DIFF_HEADS):
                h, t = u // 2, u % 2
                if u + 1 < 2 * DIFF_HEADS:
                    diff_scores(u + 1)
                b = 6 + h % 2
                pe.wait_ge(da["a"], u + 1)
                if u:
                    pe.wait_ge(da["at"], u)
                if t == 0 and h >= 2:
                    pe.wait_ge(da["on"], h - 1)
                for k in range(t + 1):
                    last = nc.tensor.transpose(ps[:, b, k * P:(k + 1) * P], d_a[:, u % 2, k * P:(k + 1) * P], ident)
                last.then_inc(da["t"], 1)
                pe.wait_ge(da["at"], u + 1)
                for k in range(t + 1):
                    last = mm(ps[:, b, T + t * P:T + (t + 1) * P], d_v[:, k, h * P:(h + 1) * P], d_at[:, u % 2, k * P:(k + 1) * P],
                              start=k == 0, stop=k == t)
                last.then_inc(da["o"], 1)
                if t == 0 and h:
                    pe.wait_ge(da["sq"], h)
                    mm(ps[:, h % 2, T:2 * T], ones[:], d_sq[:, (h - 1) % 2], start=True, stop=True).then_inc(da["n"], 1)
            pe.wait_ge(da["sq"], DIFF_HEADS)
            mm(ps[:, DIFF_HEADS % 2, T:2 * T], ones[:], d_sq[:, (DIFF_HEADS - 1) % 2], start=True, stop=True).then_inc(da["n"], 1)
            pe.wait_ge(da["r"], DIFF_HEADS)
            chunks(C_DO, 8, XB, 6)
            mlp(C_M1, 3, 7, 3)

            chunk(C_CONV, C_CONV, XA, 4)
            stats(4, True)
            wdt = par[:, PCOL["w_dt"]:PCOL["w_dt"] + KC * SSD_HEADS].rearrange("p (k r) -> p k r", k=KC)
            for t in range(NT):
                at = slice(t * P, (t + 1) * P)
                for k in range(KC):
                    mm(ps[:, 4, t * SSD_HEADS:(t + 1) * SSD_HEADS], XA.hi[:, k, at].bitcast(F32), wdt[:, k], start=k == 0, stop=False)
                    last = mm(ps[:, 4, t * SSD_HEADS:(t + 1) * SSD_HEADS], XA.lo[:, k, at].bitcast(F32), wdt[:, k],
                              start=False, stop=k == KC - 1)
            last.then_inc(sa["dt"], 1)
            chunks(C_CONV + 1, 7, XA, None)
            for c0, n in ((C_CONV + 8, 1), (C_XBC, 3), (C_Z, 2)):
                with pe.Fori(0, n) as r:
                    for j in range(8):
                        chunk(c0 + 8 * r + j, c0 + j, XA, None)
            pe.wait_ge(sa["da"], 1)
            da_m = s_small[:, 6]
            for t in range(NT):
                at = slice(t * SSD_HEADS, (t + 1) * SSD_HEADS)
                mm(ps[:, 4, 128 + t * SSD_HEADS:128 + (t + 1) * SSD_HEADS], upto_m, da_m[:, at], start=True, stop=True)
            last = mm(ps[:, 4, 256:256 + SSD_HEADS], ones[:], da_m[:, 0:SSD_HEADS], start=True, stop=True)
            last.then_inc(sa["cs"], 1)
            pe.wait_ge(ca["tap"], KC * TAPS)
            for k in range(KC):
                last = mm(ps[:, 5, 0:T], ones[:], c_out[:, k], start=k == 0, stop=k == KC - 1)
            last.then_inc(ca["mean"], 1)
            pe.wait_ge(ca["sq"], 1)
            for k in range(KC):
                last = mm(ps[:, 5, T:2 * T], ones[:], c_in[:, k, 0:T], start=k == 0, stop=k == KC - 1)
            last.then_inc(ca["var"], 1)

            for n in range(KC):
                chunk(C_YA + 2 * n, C_YA + 2 * n, XA, None)
                chunk(C_YA + 2 * n + 1, C_YA + 2 * n + 1, XB, 11 if n == 0 else None)

            def ssd_group(g):
                Bm, Cm = s_xbc[:, 16 + g], s_xbc[:, 20 + g]
                if g:
                    pe.wait_ge(sa["cbs"], g)
                for i, (s, l) in enumerate(((0, 0), (1, 1), (0, 1))):
                    last = mm(ps[:, 7, i * P:(i + 1) * P], Bm[:, s * P:(s + 1) * P], Cm[:, l * P:(l + 1) * P], start=True, stop=True)
                last.then_inc(sa["cb"], 1)
                for t in range(NT):
                    if g or t:
                        pe.wait_ge(sa["xd"], 3 * g + 2 * t)
                    if g and t == 0:
                        pe.wait_ge(sa["r"], g)
                    for k in range(4):
                        last = nc.tensor.transpose(ps[:, 4, k * P:(k + 1) * P], s_xbc[:, 4 * g + k, t * P:(t + 1) * P], ident)
                    last.then_inc(sa["x"], 1)

                def quad(q, t):
                    n = (2 * g + q) * NT + t
                    if n:
                        pe.wait_ge(sa["e"], n)
                    for i in range(4):
                        h = 8 * g + 4 * q + i
                        mm(ps[:, 5, i * P:(i + 1) * P], da_m[:, t * SSD_HEADS + h:t * SSD_HEADS + h + 1].to_broadcast([P, P]), upto_m,
                           start=True, stop=False)
                        last = mm(ps[:, 5, i * P:(i + 1) * P], later_b[:], ident_b[:], start=False, stop=True)
                    last.then_inc(sa["c"], 1)

                for q in range(2):
                    for t in range(NT):
                        quad(q, t)
                        n = (2 * g + q) * NT + t
                        pe.wait_ge(sa["sc"], n + 1)
                        pe.wait_ge(sa["xd"], 3 * g + 3)
                        if n >= 2 and t == 0:
                            pe.wait_ge(sa["yd"], 2 * (2 * g + q))
                        for i in range(4):
                            half = slice(64 * (i % 2), 64 * (i % 2) + 64)
                            ch = i // 2
                            last = mm(ps[half, 6, ch * T + t * P:ch * T + (t + 1) * P],
                                      s_xd[:, g % 2, t, (4 * q + i) * 64:(4 * q + i + 1) * 64], s_sc[:, n % 2, i * P:(i + 1) * P],
                                      start=True, stop=True)
                        if t == 1:
                            for ch in range(2):
                                cc = 2 * q + ch
                                mm(ps[:, 0 + ch, T:T + P], s_xd2[:, g % 2, cc * P:(cc + 1) * P], s_cb[:, 2], start=True, stop=True)
                                h = 8 * g + 2 * cc
                                for i in range(2):
                                    col = da_m[:, SSD_HEADS + h + i:SSD_HEADS + h + i + 1].to_broadcast([P, 64])
                                    last = mm(ps[64 * i:64 * i + 64, 2 + ch, T:T + P], col, upto_m, start=True, stop=True)
                            last.then_inc(sa["y"], 1)
                for k in range(4):
                    n = 4 * g + k
                    pe.wait_ge(sa["sq"], n + 1)
                    last = mm(ps[:, 4, 0:T], ones[:], s_sq[:, n % 2], start=k == 0, stop=k == 3)
                    last.then_inc(sa["n"], 1)

            pe.wait_ge(sa["bias"], 1)
            ssd_group(0)
            ssd_group(1)
            for n in range(KC):
                chunk(C_YB0 + 2 * n, C_YB0 + 2 * n, XA, None)
                chunk(C_YB0 + 2 * n + 1, C_YB0 + 2 * n + 1, XB, 12 if n == 0 else None)
            ssd_group(2)
            ssd_group(3)
            chunks(C_YB1, 8, XB, 13)

            for n in range(11):
                if n < 10:
                    chunk(C_SWA + n, C_SWA + n, XA, None)
                if n:
                    head_sums(16 + n - 1)
            for n in range(10, 12):
                chunk(C_SWA + n, C_SWA + n, XA, None, token_major=True)
            pe.wait_ge(hn_out, 26)
            for g in range(SWA_KV):
                for i in range(2):
                    last = mm(ps[64 * i:64 * i + 64, 6 + g // 2, g % 2 * T:(g % 2 + 1) * T], ident[:, 64 * (g % 2):64 * (g % 2) + 64],
                              w_k2[:, g // 2], start=True, stop=True)
            last.then_inc(wa["dup"], 1)

            def swa_scores(u):
                p, t = u // 2, u % 2
                if u == 0:
                    pe.wait_ge(wa["kd"], 1)
                if u >= 2:
                    pe.wait_ge(wa["ss"], u - 1)
                for i in range(2):
                    rows = slice(64 * i, 64 * i + 64)
                    last = mm(swa_scores_at(u)[:, i, 0:(t + 1) * P], w_q[rows, p, t * P:(t + 1) * P], w_kd[rows, p // 2, 0:(t + 1) * P],
                              start=True, stop=True)
                last.then_inc(wa["s"], 1)

            pe.wait_ge(bank_free, C_YC)
            swa_scores(0)
            for u in range(2 * SWA_PAIRS):
                p, t = u // 2, u % 2
                if u + 1 < 2 * SWA_PAIRS:
                    swa_scores(u + 1)
                pe.wait_ge(wa["r"], u + 1)
                if u:
                    pe.wait_ge(wa["pt"], u)
                for i in range(2):
                    for k in range(t + 1):
                        last = nc.tensor.transpose(ps[:, 6, (2 * i + k) * P:(2 * i + k + 1) * P], w_p[:, u % 2, i, k * P:(k + 1) * P], ident)
                last.then_inc(wa["t"], 1)
                pe.wait_ge(wa["pt"], u + 1)
                if t == 0 and p >= 2:
                    pe.wait_ge(XB.lo_done, KC * 14 + p - 1)
                    pe.wait_ge(XB.bf_done, KC * 14 + p - 1)
                for i in range(2):
                    half = slice(64 * i, 64 * i + 64)
                    for k in range(t + 1):
                        last = mm(ps[half, OUT_BANKS[p % 2], t * P:(t + 1) * P], w_v[:, k, p // 2 * 64:p // 2 * 64 + 64],
                                  w_pt[:, u % 2, i, k * P:(k + 1) * P], start=k == 0, stop=k == t)
                if t == 1:
                    last.then_inc(wa["o"], 1)
            for n in range(KC):
                chunk(C_YC + 2 * n, C_YC + 2 * n, XA, None)
                chunk(C_YC + 2 * n + 1, C_YC + 2 * n + 1, XB, 14 if n == 0 else None)
            chunks(C_MIX, 8, XB, 15)

            def pair_sums(k):
                pe.wait_ge(xa["sq"], k + 1)
                if k >= 2:
                    pe.wait_ge(xa["r"], k - 1)
                for i in range(2):
                    last = mm(ps[:, 4 + k % 2, 0:T], ones[:], x_sq[:, k % 2, i], start=i == 0, stop=i == 1)
                last.then_inc(xa["mm"], 1)

            for n in range(9):
                if n < 8:
                    chunk(C_XK + n, C_XK + n, XA, 5 if n == 0 else None)
                    if n == 0:
                        stats(5, True)
                if n and n % 2 == 0:
                    pair_sums(n // 2 - 1)
            chunks(C_XV, 8, XA, None, token_major=True)
            for n in range(9):
                if n < 8:
                    chunk(C_XQ + n, C_XQ + n, XB, 16 if n == 0 else None)
                    if n == 0:
                        stats(6, False)
                if n and n % 2 == 0:
                    pair_sums(4 + n // 2 - 1)

            def x_scores(h):
                if h == 0:
                    pe.wait_ge(xa["out"], 16)
                if h >= 2:
                    pe.wait_ge(xa["p"], h - 1)
                for t in range(NT):
                    for i in range(2):
                        last = mm(ps[:, 4 + h % 2, t * T:(t + 1) * T], x_q[:, 2 * h + i, t * P:(t + 1) * P], x_k[:, 2 * h + i],
                                  start=i == 0, stop=i == 1)
                last.then_inc(xa["s"], 1)

            x_scores(0)
            for h in range(X_HEADS):
                if h + 1 < X_HEADS:
                    x_scores(h + 1)
                pe.wait_ge(xa["n"], h + 1)
                if h:
                    pe.wait_ge(xa["pt"], h)
                for k in range(2):
                    for t in range(NT):
                        last = nc.tensor.transpose(ps[:, 6, k * T + t * P:k * T + (t + 1) * P], x_p[:, h % 2, t, k * P:(k + 1) * P], ident)
                last.then_inc(xa["t"], 1)
                pe.wait_ge(xa["pt"], h + 1)
                if h >= 2:
                    pe.wait_ge(XB.lo_done, KC * 17 + 2 * h - 2)
                    pe.wait_ge(XB.bf_done, KC * 17 + 2 * h - 2)
                for half in range(2):
                    f = slice(h * T + half * P, h * T + (half + 1) * P)
                    for k in range(2):
                        last = mm(ps[:, OUT_BANKS[h % 2], half * T:(half + 1) * T], x_v[:, k, f], x_pt[:, h % 2, k], start=k == 0, stop=k == 1)
                last.then_inc(xa["o"], 1)
            chunks(C_XO, 8, XB, 17)
            mlp(C_M2, 6, 18, 7)

        @block.scalar
        def _(act):
            A = nc.scalar.activation
            step = [0]

            def done(ins):
                ins.then_inc(act_step, 1)
                step[0] += 1
                act.wait_ge(act_step, step[0])

            def cut_hi(c, j):
                if isinstance(c, int) and c >= CHUNKS:
                    return
                if j % 2 == 0:
                    if isinstance(c, int):
                        act.wait_ge(slab_in[j // 2 % RING], 16 * (c // 2 // RING + 1))
                    else:
                        act.wait_ge(slab_in[j // 2 % RING], 2 * (c - j % 8) + 16)
                if not isinstance(c, int) or c >= HI_SLOTS:
                    act.wait_ge(gemm_done, c - HI_SLOTS + 1)
                nc.scalar.copy(w_hi[:, j % HI_SLOTS].rearrange("p k n -> p (k n)"),
                               raw[:, j // 2 % RING, j % 2]).then_inc(hi_done, 1)

            def operand(X, build, k, src, gain=None):
                if gain is None:
                    nc.scalar.copy(X.hi[:, k], src).then_inc(X.hi_done, 1)
                    nc.scalar.copy(X.bf[:, k], src).then_inc(X.bf_done, 1)
                else:
                    A(X.hi[:, k], src, ACT.Copy, scale=gain).then_inc(X.hi_done, 1)
                    A(X.bf[:, k], src, ACT.Copy, scale=gain).then_inc(X.bf_done, 1)

            def rms(nu, to, to_tok=None):
                act.wait_ge(stat_mm, nu + 1)
                if to_tok is not None:
                    A(lnt_tok[:], stat_tok(), ACT.Ln, bias=eps[:, 0:1], scale=1.0 / D)
                done(A(lnt[:, 0], stat_rstd(), ACT.Ln, bias=eps[:, 0:1], scale=1.0 / D))
                if to_tok is not None:
                    A(to_tok[:], lnt_tok[:], ACT.Exp, scale=-0.5)
                A(to[:], lnt[:, 0], ACT.Exp, scale=-0.5).then_inc(rstd_done, 1)

            def head_sq(k, c, src):
                act.wait_ge(bank_free, c + 1)
                if k >= 2:
                    act.wait_ge(hn_mm, k - 1)
                A(hn_sqb[:, k % 2], src, ACT.Square).then_inc(hn_sq, 1)

            def head_rstd(k):
                act.wait_ge(hn_mm, k + 1)
                A(lnt[:, k % 2], ps[:, 4 + k % 2, 0:T], ACT.Ln, bias=eps[:, 0:1], scale=1.0 / 64).then_inc(hn_ln, 1)
                act.wait_ge(hn_ln, k + 1)
                if k >= 2:
                    act.wait_ge(hn_out, k - 1)
                A(hn_rb[:, k % 2], lnt[:, k % 2], ACT.Exp, scale=-0.5).then_inc(hn_r, 1)

            def residual(c0, X, build, gain):
                for n in range(8):
                    cut_hi(c0 + n + AHEAD, c0 + n + AHEAD)
                    if X is not None:
                        act.wait_ge(bank_free, c0 + n + 1)
                        operand(X, build, n, H[:, n], pcol(gain, n))

            def mlp(c0, m, nu, X, build, gain):
                o = c0 % 8

                def group(g, first, last):
                    c = c0 + 16 * g
                    for j in range(8):
                        cut_hi(c + j + AHEAD, o + j + AHEAD)
                        if first and j == 0:
                            rms(nu, rstd)
                        act.wait_ge(sq_done, 32 * m + 8 * g + j + 1)
                        operand(XB, None, j, m_sq[:, j % 2])
                    for j in range(8):
                        cut_hi(c + 8 + j + AHEAD, o + j + AHEAD)
                        if last and X is not None:
                            act.wait_ge(bank_free, c + 8 + j + 1)
                            operand(X, build, j, H[:, j], pcol(gain, j))
                group(0, True, False)
                with act.Fori(1, HID_GROUPS - 1) as g:
                    group(g, False, False)
                group(HID_GROUPS - 1, False, True)

            act.wait_ge(in_done, 16)
            act.wait_ge(par_done, 16)
            for k in range(KC):
                operand(XA, 0, k, H[:, k], pcol("a_norm", k))
                if k < AHEAD:
                    cut_hi(k, k)
            act.wait_ge(con_done, 16)
            nc.scalar.copy(ident_b[:], ident).then_inc(bf_set, 1)
            A(later_b[:], after_m, ACT.Copy, scale=NEG).then_inc(bf_set, 1)

            for n in range(8):
                cut_hi(n + AHEAD, n + AHEAD)
                if n == 0:
                    act.wait_ge(set_done, 1)
                    rms(0, rstd, rtok)
            for t in range(NT):
                act.wait_ge(ga["logit"], t + 1)
                done(A(g_lt[:, t], ps[:, 4 + t, :], ACT.Abs))
                done(A(g_lt[:, t], g_lt[:, t], ACT.Exp, scale=-1.0))
                A(g_lt[:, t], g_lt[:, t], ACT.Ln, bias=one[:, 0:1]).then_inc(ga["sp"], 1)
            for u in range(2 * GLA_HEADS):
                for c in (8 + 2 * u, 9 + 2 * u):
                    cut_hi(c + AHEAD, c + AHEAD)
                act.wait_ge(ga["d"], u + 1)
                if u >= 2:
                    act.wait_ge(ga["s"], u - 1)
                A(g_ke[:, u % 2], ps[:, 4:6, :].rearrange("p a b -> p (a b)"), ACT.Exp, scale=1.0 / GLA_TAU).then_inc(ga["e"], 1)
            act.wait_ge(bank_free, C_GO)
            A(g_gate.rearrange("p a b -> p (a b)"), g_gate.rearrange("p a b -> p (a b)"), ACT.Silu).then_inc(ga["silu"], 1)
            for h in range(GLA_HEADS + 2):
                if h < GLA_HEADS:
                    act.wait_ge(ga["o"], h + 1)
                    if h >= 2:
                        act.wait_ge(ga["n"], h - 1)
                    A(g_sq[:, h % 2].rearrange("p a b -> p (a b)"), ps[:, 4 + h % 2, :], ACT.Square).then_inc(ga["sq"], 1)
                if 1 <= h <= GLA_HEADS:
                    i = h - 1
                    act.wait_ge(ga["n"], i + 1)
                    done(A(lnt[:, i % 2], ps[:, 6 + i % 2, 0:T], ACT.Ln, bias=eps[:, 0:1], scale=1.0 / 256))
                    if i >= 2:
                        act.wait_ge(ga["on"], 2 * (i - 1))
                    A(g_ro[:, i % 2], lnt[:, i % 2], ACT.Exp, scale=-0.5).then_inc(ga["r"], 1)
                if h >= 2:
                    i = h - 2
                    act.wait_ge(ga["on"], 2 * i + 2)
                    for half in range(2):
                        operand(XB, 0, 2 * i + half, g_on[:, i % 2, half])
            residual(C_GO, XA, 1, "mlp_norm0")
            mlp(C_M0, 0, 1, XA, 2, "kv_norm")

            act.wait_ge(gemm_done, C_DK)
            for k in range(KC):
                operand(XB, 5, k, H[:, k], pcol("b_norm", k))
            for n in range(9):
                if n < 8:
                    cut_hi(C_DK + n + AHEAD, C_DK + n + AHEAD)
                    if n == 0:
                        rms(2, rstd, rtok)
                    head_sq(n, C_DK + n, d_k[:, n])
                if n:
                    head_rstd(n - 1)
            for n in range(8):
                cut_hi(C_DV + n + AHEAD, C_DV + n + AHEAD)
            for n in range(9):
                if n < 8:
                    cut_hi(C_DQ + n + AHEAD, C_DQ + n + AHEAD)
                    head_sq(8 + n, C_DQ + n, d_q[:, n])
                if n:
                    head_rstd(8 + n - 1)
            act.wait_ge(da["lam"], 1)
            A(d_lam[:, 2:4], d_lam[:, 0:2], ACT.Exp).then_inc(da["lame"], 1)

            def diff_exp(u):
                t = u % 2
                act.wait_ge(da["max"], u + 1)
                if u >= 2:
                    act.wait_ge(da["a"], u - 1)
                for c in range(2):
                    ins = A(d_p[:, u % 2, c, 0:(t + 1) * P], diff_scores_at(u)[:, c, 0:(t + 1) * P], ACT.Exp,
                            bias=d_st[:, u % 2, c:c + 1], accum_out=d_st[:, u % 2, 2 + c:3 + c])
                ins.then_inc(da["p"], 1)

            diff_exp(0)
            for u in range(2 * DIFF_HEADS):
                h, t = u // 2, u % 2
                if u + 1 < 2 * DIFF_HEADS:
                    diff_exp(u + 1)
                act.wait_ge(da["t"], u + 1)
                if u >= 2:
                    act.wait_ge(da["o"], u - 1)
                nc.scalar.copy(d_at[:, u % 2, 0:(t + 1) * P], ps[:, 6 + h % 2, 0:(t + 1) * P]).then_inc(da["at"], 1)
                if t == 1:
                    act.wait_ge(da["o"], u + 1)
                    if h >= 2:
                        act.wait_ge(da["n"], h - 1)
                    A(d_sq[:, h % 2], ps[:, 6 + h % 2, T:2 * T], ACT.Square).then_inc(da["sq"], 1)
                if t == 0 and h:
                    i = h - 1
                    act.wait_ge(da["n"], i + 1)
                    done(A(lnt[:, i % 2], ps[:, (i + 1) % 2, T:2 * T], ACT.Ln, bias=eps[:, 0:1], scale=1.0 / P))
                    if i >= 2:
                        act.wait_ge(da["on"], i - 1)
                    A(d_ro[:, i % 2], lnt[:, i % 2], ACT.Exp, scale=-0.5).then_inc(da["r"], 1)
                    act.wait_ge(da["on"], i + 1)
                    operand(XB, 6, i, d_on[:, i % 2])
            i = DIFF_HEADS - 1
            act.wait_ge(da["n"], i + 1)
            done(A(lnt[:, i % 2], ps[:, (i + 1) % 2, T:2 * T], ACT.Ln, bias=eps[:, 0:1], scale=1.0 / P))
            A(d_ro[:, i % 2], lnt[:, i % 2], ACT.Exp, scale=-0.5).then_inc(da["r"], 1)
            act.wait_ge(da["on"], i + 1)
            operand(XB, 6, i, d_on[:, i % 2])
            residual(C_DO, XA, 3, "mlp_norm1")
            mlp(C_M1, 1, 3, XA, 4, "norm_mix")

            cut_hi(C_CONV + AHEAD, C_CONV + AHEAD)
            rms(4, rstd, rtok)
            act.wait_ge(sa["dtx"], 1)
            done(A(s_small[:, 1], s_small[:, 0], ACT.Abs))
            done(A(s_small[:, 2], s_small[:, 1], ACT.Exp, scale=-1.0))
            A(s_small[:, 4, 0:SSD_HEADS], pcol("A_log", 0, SSD_HEADS), ACT.Exp)
            A(s_small[:, 3], s_small[:, 2], ACT.Ln, bias=one[:, 0:1]).then_inc(sa["dta"], 1)
            for n in range(16):
                if n:
                    cut_hi(C_CONV + n + AHEAD, C_CONV + n + AHEAD)
                if n % 2:
                    act.wait_ge(bank_free, C_CONV + n + 1)
                    i = n // 2
                    A(c_tmp[:, i % 2], c_tmp[:, i % 2], ACT.Sigmoid).then_inc(ca["sig"], 1)
            for n in range(24):
                c = C_XBC + n
                cut_hi(c + AHEAD, c + AHEAD)
                act.wait_ge(sa["tap"], SSD_TAPS * (n + 1))
                A(s_xbc[:, n], s_tap[:, n % 2], ACT.Silu, bias=pcol("ssd_conv_b", n)).then_inc(sa["silu"], 1)
            with act.Fori(0, 2) as r:
                for j in range(8):
                    c = C_Z + 8 * r + j
                    cut_hi(c + AHEAD, C_Z + j + AHEAD)
                    act.wait_ge(bank_free, c + 1)
                    z = s_z[:, bass.ds(8 * r + j, 1)].rearrange("p o t -> p (o t)")
                    A(z, z, ACT.Silu).then_inc(sa["z"], 1)
            act.wait_ge(sa["bias"], 1)
            A(s_small[:, 9, 0:SSD_HEADS], s_small[:, 8, 0:SSD_HEADS], ACT.Exp).then_inc(sa["dte"], 1)
            act.wait_ge(ca["xc"], 1)
            for k in range(KC):
                ins = A(c_in[:, k, 0:T], c_out[:, k], ACT.Square)
            ins.then_inc(ca["sq"], 1)
            act.wait_ge(ca["var"], 1)
            done(A(lnt[:, 0], ps[:, 5, T:2 * T], ACT.Ln, bias=eps[:, 0:1], scale=1.0 / D))
            A(lnt[:, 1], lnt[:, 0], ACT.Exp, scale=-0.5).then_inc(ca["r"], 1)
            act.wait_ge(ca["norm"], 1)
            for k in range(KC):
                A(c_out[:, k], c_out[:, k], ACT.Silu, bias=pcol("ln_b", k), scale=pcol("ln_g", k)).then_inc(ca["silu"], 1)
            for k in range(KC):
                act.wait_ge(ca["silu"], k + 1)
                operand(XB, 11, k, c_out[:, k])

            def gate(c0, branch, n, to):
                cut_hi(c0 + 2 * n + AHEAD, c0 + 2 * n + AHEAD)
                act.wait_ge(bank_free, c0 + 2 * n + 1)
                A(to, y_tmp[:, n % 2], ACT.Sigmoid, bias=pcol("gate_bias", KC * branch + n)).then_inc(gate_done, 1)
                cut_hi(c0 + 2 * n + 1 + AHEAD, c0 + 2 * n + 1 + AHEAD)

            for n in range(KC):
                if n >= 2:
                    act.wait_ge(bank_free, C_YA + 2 * (n - 2) + 2)
                gate(C_YA, 0, n, y_gate[:, n % 2])

            def ssd_group(g):
                for i in range(3):
                    if i == 0:
                        act.wait_ge(sa["cb"], g + 1)
                        if g:
                            act.wait_ge(sa["y"], 2 * g)
                    ins = nc.scalar.copy(s_cb[:, i], ps[:, 7, i * P:(i + 1) * P])
                ins.then_inc(sa["cbs"], 1)
                for q in range(2):
                    for t in range(NT):
                        n = (2 * g + q) * NT + t
                        act.wait_ge(sa["c"], n + 1)
                        if n >= 2:
                            act.wait_ge(sa["sc"], n - 1)
                        for i in range(4):
                            h = t * SSD_HEADS + 8 * g + 4 * q + i
                            ins = A(s_e[:, n % 2, i * P:(i + 1) * P], ps[:, 5, i * P:(i + 1) * P], ACT.Exp, bias=s_small[:, 7, h:h + 1])
                        ins.then_inc(sa["e"], 1)
                    act.wait_ge(sa["y"], 2 * g + q + 1)
                    if 2 * g + q:
                        act.wait_ge(sa["yd"], 2 * (2 * g + q))
                    for ch in range(2):
                        ins = A(s_eb[:, ch], ps[:, 2 + ch, T:T + P], ACT.Exp)
                    ins.then_inc(sa["eb"], 1)
                    for ch in range(2):
                        n = 4 * g + 2 * q + ch
                        act.wait_ge(sa["yd"], n + 1)
                        if n >= 2:
                            act.wait_ge(sa["n"], n - 1)
                        A(s_sq[:, n % 2], s_xbc[:, n], ACT.Square).then_inc(sa["sq"], 1)
                act.wait_ge(sa["n"], 4 * g + 4)
                done(A(lnt[:, 0], ps[:, 4, 0:T], ACT.Ln, bias=eps[:, 0:1], scale=1.0 / 512))
                if g:
                    act.wait_ge(sa["on"], 4 * g)
                A(s_rg[:], lnt[:, 0], ACT.Exp, scale=-0.5).then_inc(sa["r"], 1)
                for k in range(4):
                    act.wait_ge(sa["on"], 4 * g + k + 1)
                    operand(XB, 12 + g // 2, 4 * (g % 2) + k, s_xbc[:, 4 * g + k])

            act.wait_ge(gemm_done, C_YB0)
            ssd_group(0)
            ssd_group(1)
            for n in range(KC):
                gate(C_YB0, 1, n, gate_b[:, n])
            act.wait_ge(gemm_done, C_YB1)
            ssd_group(2)
            ssd_group(3)
            for n in range(8):
                cut_hi(C_YB1 + n + AHEAD, C_YB1 + n + AHEAD)

            for n in range(11):
                if n < 10:
                    cut_hi(C_SWA + n + AHEAD, C_SWA + n + AHEAD)
                    head_sq(16 + n, C_SWA + n, w_q[:, n] if n < 8 else w_k2[:, n - 8])
                if n:
                    head_rstd(16 + n - 1)
            for n in range(10, 12):
                cut_hi(C_SWA + n + AHEAD, C_SWA + n + AHEAD)
            act.wait_ge(wa["dup"], 1)
            nc.scalar.copy(w_kd.rearrange("p a b -> p (a b)"), ps[:, 6:8, :].rearrange("p a b -> p (a b)")).then_inc(wa["kd"], 1)

            def swa_exp(u):
                t = u % 2
                act.wait_ge(wa["m"], u + 1)
                if u >= 2:
                    act.wait_ge(wa["t"], u - 1)
                for i in range(2):
                    A(w_p[:, u % 2, i, 0:(t + 1) * P], w_s[:, u % 2, i, 0:(t + 1) * P], ACT.Exp, bias=w_st[:, u % 2, 2 + i:3 + i],
                      accum_out=w_st[:, u % 2, 4 + i:5 + i])
                A(w_st[:, u % 2, 8:10], w_st[:, u % 2, 6:8], ACT.Exp).then_inc(wa["p"], 1)

            swa_exp(0)
            for u in range(2 * SWA_PAIRS):
                p, t = u // 2, u % 2
                if u + 1 < 2 * SWA_PAIRS:
                    swa_exp(u + 1)
                act.wait_ge(wa["t"], u + 1)
                if u >= 2:
                    act.wait_ge(wa["o"], u // 2)
                for i in range(2):
                    ins = nc.scalar.copy(w_pt[:, u % 2, i, 0:(t + 1) * P], ps[:, 6, 2 * i * P:(2 * i + t + 1) * P])
                ins.then_inc(wa["pt"], 1)
                if t == 1:
                    act.wait_ge(wa["o"], p + 1)
                    if p == 0:
                        act.wait_ge(gemm_done, C_SWA)
                    operand(XB, 14, p, ps[:, OUT_BANKS[p % 2], 0:T])
            for n in range(KC):
                if n >= 2:
                    act.wait_ge(bank_free, C_YC + 2 * (n - 2) + 2)
                gate(C_YC, 2, n, y_gate[:, n % 2])
            act.wait_ge(gemm_done, C_MIX)
            act.wait_ge(bank_free, C_MIX)
            for k in range(KC):
                act.wait_ge(merged_done, 2 * KC + k + 1)
                operand(XB, 15, k, merged[:, k])
            act.wait_ge(mem_in, 16)
            for k in range(KC):
                operand(XA, 5, k, x_mem[:, k], pcol("norm_mem", k))
            residual(C_MIX, None, None, None)
            act.wait_ge(bank_free, C_MIX + 8)
            for k in range(KC):
                operand(XB, 16, k, H[:, k], pcol("norm_xattn", k))

            def pair_sq(k, c, src):
                act.wait_ge(bank_free, c + 1)
                if k >= 2:
                    act.wait_ge(xa["mm"], k - 1)
                A(x_sq[:, k % 2].rearrange("p a b -> p (a b)"), src.rearrange("p a b -> p (a b)"), ACT.Square).then_inc(xa["sq"], 1)

            def pair_rstd(k):
                act.wait_ge(xa["mm"], k + 1)
                done(A(lnt[:, k % 2], ps[:, 4 + k % 2, 0:T], ACT.Ln, bias=eps[:, 0:1], scale=1.0 / 256))
                if k >= 2:
                    act.wait_ge(xa["out"], 2 * (k - 1))
                A(x_rk[:, k % 2], lnt[:, k % 2], ACT.Exp, scale=-0.5).then_inc(xa["r"], 1)

            for n in range(10):
                if n < 8:
                    cut_hi(C_XK + n + AHEAD, C_XK + n + AHEAD)
                    if n == 0:
                        rms(5, rstd_mem, rtok_mem)
                    if n % 2:
                        pair_sq(n // 2, C_XK + n, x_k[:, n - 1:n + 1])
                if n >= 2 and n % 2 == 0:
                    pair_rstd(n // 2 - 1)
            for n in range(8):
                cut_hi(C_XV + n + AHEAD, C_XV + n + AHEAD)
            for n in range(10):
                if n < 8:
                    cut_hi(C_XQ + n + AHEAD, C_XQ + n + AHEAD)
                    if n == 0:
                        rms(6, rstd)
                    if n % 2:
                        pair_sq(4 + n // 2, C_XQ + n, x_q[:, n - 1:n + 1])
                if n >= 2 and n % 2 == 0:
                    pair_rstd(4 + n // 2 - 1)

            def x_exp(h):
                act.wait_ge(xa["max"], h + 1)
                if h >= 2:
                    act.wait_ge(xa["t"], h - 1)
                for t in range(NT):
                    ins = A(x_p[:, h % 2, t], ps[:, 4 + h % 2, t * T:(t + 1) * T], ACT.Exp, bias=x_st[:, h % 2, t:t + 1],
                            accum_out=x_st[:, h % 2, 2 + t:3 + t])
                ins.then_inc(xa["p"], 1)

            x_exp(0)
            for h in range(X_HEADS):
                if h + 1 < X_HEADS:
                    x_exp(h + 1)
                act.wait_ge(xa["t"], h + 1)
                if h >= 2:
                    act.wait_ge(xa["o"], h - 1)
                nc.scalar.copy(x_pt[:, h % 2].rearrange("p a b -> p (a b)"), ps[:, 6, :]).then_inc(xa["pt"], 1)
                act.wait_ge(xa["o"], h + 1)
                for half in range(2):
                    operand(XB, 17, 2 * h + half, ps[:, OUT_BANKS[h % 2], half * T:(half + 1) * T])
            residual(C_XO, XA, 6, "norm_mlp2")
            mlp(C_M2, 2, 7, None, None, None)
            for n in range(KC):
                act.wait_ge(bank_free, C_M2 + 56 + n + 1)
                act.dma_start(out_d[:, n], H[:, n]).then_inc(out_done, 16)
            act.wait_ge(out_done, 16 * KC)

        @block.vector
        def _(dve):
            V = nc.vector
            TT, TS, STT = V.tensor_tensor, V.tensor_scalar, V.scalar_tensor_tensor
            step = [0]

            def done(ins):
                ins.then_inc(dve_step, 1)
                step[0] += 1
                dve.wait_ge(dve_step, step[0])

            def cut_lo(c, j):
                if isinstance(c, int) and c >= CHUNKS:
                    return
                dve.wait_ge(hi_done, c + 1)
                TT(w_lo[:, j % HI_SLOTS].rearrange("p k n -> p (k n)"), raw[:, j // 2 % RING, j % 2],
                   w_hi[:, j % HI_SLOTS].rearrange("p k n -> p (k n)").bitcast(F32), ALU.subtract).then_inc(lo_done, 1)

            def got(c, j):
                dve.wait_ge(gemm_done, c + 1)
                return ps[:, j % BANKS, 0:T]

            def operand_lo(X, n, k, src, gain=None):
                dve.wait_ge(X.hi_done, n)
                hi = X.hi[:, k].bitcast(F32)
                if gain is None:
                    TT(X.lo[:, k], src, hi, ALU.subtract).then_inc(X.lo_done, 1)
                else:
                    STT(X.lo[:, k], src, gain, hi, ALU.mult, ALU.subtract).then_inc(X.lo_done, 1)

            def scaled(c, j, to):
                TT(to, got(c, j), rstd[:], ALU.mult).then_inc(bank_free, 1)

            def tokens(c, j, to, r):
                dve.wait_ge(gemm_done, c + 1)
                for t in range(NT):
                    ins = TS(to[:, t], ps[:, j % BANKS, t * P:(t + 1) * P], r[:, t:t + 1], None, ALU.mult)
                ins.then_inc(bank_free, 1)

            def residual(c0, X, build, gain):
                for n in range(8):
                    c = c0 + n
                    cut_lo(c + AHEAD, c + AHEAD)
                    TT(H[:, n], got(c, c), H[:, n], ALU.add).then_inc(bank_free, 1)
                    if X is not None and n:
                        operand_lo(X, KC * build + n, n - 1, H[:, n - 1], pcol(gain, n - 1))
                if X is not None:
                    operand_lo(X, KC * build + 8, 7, H[:, 7], pcol(gain, 7))

            def head_out(k, x, gain):
                dve.wait_ge(hn_r, k + 1)
                STT(x, x, gain, hn_rb[:, k % 2], ALU.mult, ALU.mult).then_inc(hn_out, 1)

            def mlp(c0, m, nu, xb_build0, X, build, gain):
                o = c0 % 8

                def group(g, first, last):
                    c = c0 + 16 * g
                    n0 = KC * (xb_build0 + g)
                    for j in range(8):
                        cut_lo(c + j + AHEAD, o + j + AHEAD)
                        if first and j == 0:
                            dve.wait_ge(rstd_done, nu + 1)
                        i = 32 * m + 8 * g + j
                        if not isinstance(i, int) or i >= 2:
                            dve.wait_ge(sq_done, i - 1)
                        STT(m_relu[:, j % 2], got(c + j, o + j), 0.0, rstd[:], ALU.max, ALU.mult).then_inc(bank_free, 1)
                        if j:
                            operand_lo(XB, n0 + j, j - 1, m_sq[:, (j - 1) % 2])
                    for j in range(8):
                        cut_lo(c + 8 + j + AHEAD, o + j + AHEAD)
                        if j == 0:
                            operand_lo(XB, n0 + 8, 7, m_sq[:, 1])
                        TT(H[:, j], got(c + 8 + j, o + j), H[:, j], ALU.add).then_inc(bank_free, 1)
                        if last and X is not None and j:
                            operand_lo(X, KC * build + j, j - 1, H[:, j - 1], pcol(gain, j - 1))
                    if last and X is not None:
                        operand_lo(X, KC * build + 8, 7, H[:, 7], pcol(gain, 7))
                group(0, True, False)
                with dve.Fori(1, HID_GROUPS - 1) as g:
                    group(g, False, False)
                group(HID_GROUPS - 1, False, True)

            for k in range(KC):
                operand_lo(XA, k + 1, k, H[:, k], pcol("a_norm", k))
                if k < AHEAD:
                    cut_lo(k, k)

            for n in range(8):
                cut_lo(n + AHEAD, n + AHEAD)
                if n == 0:
                    dve.wait_ge(rstd_done, 1)
                if n < 4:
                    STT(g_q[:, n], got(n, n), float(P) ** -0.5, rstd[:], ALU.mult, ALU.mult).then_inc(bank_free, 1)
                else:
                    scaled(n, n, g_k[:, n - 4])
                if n == 4:
                    dve.wait_ge(ga["z"], 1)
                    dve.wait_ge(ga["zs"], 1)
                    TT(g_z[0:GLA_RANK], ps[0:GLA_RANK, 7, 0:T], rstd[0:GLA_RANK], ALU.mult).then_inc(ga["zs"], 1)
            for t in range(NT):
                dve.wait_ge(ga["sp"], t + 1)
                STT(g_la[:, t], ps[:, 4 + t, :], 0.0, g_lt[:, t], ALU.min, ALU.subtract).then_inc(ga["la"], 1)
            dve.wait_ge(mask_done, 16)

            def decayed(u):
                h, t = u // 2, u % 2
                at = slice(t * P, (t + 1) * P)
                q = g_q[:, h, at].unsqueeze(1)
                k = g_k[:, h, at].unsqueeze(1)
                e = g_ke[:, u % 2].rearrange("p (l i) -> p l i", i=P)
                qe = g_qe[:, u % 2].rearrange("p (l i) -> p l i", i=P)
                dve.wait_ge(ga["e"], u + 1)
                lo = 1 - t
                TT(qe[:, lo:lo + LEVELS], e[:, lo:lo + LEVELS], q.to_broadcast([P, LEVELS, P]), ALU.mult)
                if t == 0:
                    TT(g_kx[:, h], e[:, 0], g_k[:, h, at], ALU.mult)
                else:
                    TT(g_qx[:, h], e[:, LEVELS], g_q[:, h, at], ALU.mult)
                TT(e[:, lo:lo + LEVELS], e[:, lo:lo + LEVELS], k.to_broadcast([P, LEVELS, P]), ALU.mult).then_inc(ga["qk"], 1)

            def merge(u):
                h, t = u // 2, u % 2
                dve.wait_ge(ga["s"], u + 1)
                if u:
                    dve.wait_ge(ga["m"], u)
                done(TT(g_sm, ps[:, 6:8, :].rearrange("p a b -> p (a b)"), g_pairs, ALU.mult))
                V.tensor_reduce(g_att[:, h, t], g_sm.rearrange("p (l i) -> p i l", i=P), AX.X, ALU.add).then_inc(ga["m"], 1)

            for u in range(2 * GLA_HEADS + 2):
                if u < 2 * GLA_HEADS:
                    for c in (8 + 2 * u, 9 + 2 * u):
                        cut_lo(c + AHEAD, c + AHEAD)
                        if c < C_GG:
                            tokens(c, c, g_v[:, :, (c - C_GV) * P:(c - C_GV + 1) * P], rtok)
                        else:
                            scaled(c, c, g_gate[:, c - C_GG])
                if 1 <= u <= 2 * GLA_HEADS:
                    decayed(u - 1)
                if u >= 2:
                    merge(u - 2)
            dve.wait_ge(ga["s"], 2 * GLA_HEADS + 1)
            V.tensor_copy(g_att[:, :, 2], ps[:, 4, :].rearrange("p (h i) -> p h i", h=GLA_HEADS)).then_inc(ga["m"], 1)
            dve.wait_ge(ga["silu"], 1)
            for h in range(GLA_HEADS + 1):
                if h < GLA_HEADS:
                    dve.wait_ge(ga["r"], h + 1)
                    if h >= 2:
                        dve.wait_ge(XB.bf_done, 2 * (h - 1))
                        dve.wait_ge(XB.lo_done, 2 * (h - 1))
                    for half in range(2):
                        ins = STT(g_on[:, h % 2, half], ps[:, 4 + h % 2, half * T:(half + 1) * T], pcol("a_head_norm", half),
                                  g_ro[:, h % 2], ALU.mult, ALU.mult)
                    done(ins)
                    for half in range(2):
                        TT(g_on[:, h % 2, half], g_on[:, h % 2, half], g_gate[:, 2 * h + half], ALU.mult).then_inc(ga["on"], 1)
                if h:
                    for half in range(2):
                        operand_lo(XB, 2 * (h - 1) + half + 1, 2 * (h - 1) + half, g_on[:, (h - 1) % 2, half])
            residual(C_GO, XA, 1, "mlp_norm0")
            mlp(C_M0, 0, 1, 1, XA, 2, "kv_norm")

            for k in range(KC):
                operand_lo(XB, KC * 5 + k + 1, k, H[:, k], pcol("b_norm", k))
            TS(gains[:, 0:2], pcol("xq_norm", 0, 2), 256.0 ** -0.5, None, ALU.mult)
            TS(gains[:, 2:3], pcol("b_q_norm"), float(DIFF_DH) ** -0.5, None, ALU.mult)
            TS(gains[:, 3:4], pcol("b_head_norm"), 1.0 - LAMBDA_INIT, None, ALU.mult)
            lp = pcol("b_lambda", 0, 4 * DIFF_DH).rearrange("p (a b d) -> p a b d", a=2, b=2)
            done(TT(d_lp, lp[:, :, 0], lp[:, :, 1], ALU.mult))
            V.tensor_reduce(d_lam[:, 0:2], d_lp, AX.X, ALU.add).then_inc(da["lam"], 1)
            for n in range(10):
                if n < 8:
                    cut_lo(C_DK + n + AHEAD, C_DK + n + AHEAD)
                    if n == 0:
                        dve.wait_ge(rstd_done, 3)
                    scaled(C_DK + n, n, d_k[:, n])
                if n >= 2:
                    head_out(n - 2, d_k[:, n - 2], pcol("k_norm"))
            for h in range(SWA_HEADS):
                n = h // 2
                if h % 2 == 0:
                    cut_lo(C_DV + n + AHEAD, C_DV + n + AHEAD)
                    tokens(C_DV + n, n, d_v[:, :, n * P:(n + 1) * P], rtok)
                dve.wait_ge(band_mm, h + 1)
                if h >= 2:
                    dve.wait_ge(band_out[h % 2], 16 * (h // 2))
                V.tensor_copy(w_row[:, h % 2], ps[:, 6 + h % 2, 0:BAND]).then_inc(band_set, 1)
            for n in range(10):
                if n < 8:
                    cut_lo(C_DQ + n + AHEAD, C_DQ + n + AHEAD)
                    scaled(C_DQ + n, n, d_q[:, n])
                if n >= 2:
                    head_out(8 + n - 2, d_q[:, n - 2], gains[:, 2:3])
            dve.wait_ge(da["lame"], 1)
            done(TT(d_lam[:, 4:5], d_lam[:, 3:4], d_lam[:, 2:3], ALU.subtract))
            done(TS(d_lam[:, 5:6], d_lam[:, 4:5], -LAMBDA_INIT, None, ALU.add))

            def diff_max(u):
                t = u % 2
                dve.wait_ge(da["s"], u + 1)
                V.tensor_reduce(d_st[:, u % 2, 0:2], diff_scores_at(u)[:, :, 0:(t + 1) * P],
                                AX.X, ALU.max, negate=True).then_inc(da["max"], 1)

            def diff_head(h):
                dve.wait_ge(da["r"], h + 1)
                if h >= 2:
                    dve.wait_ge(XB.bf_done, KC * 6 + h - 1)
                    dve.wait_ge(XB.lo_done, KC * 6 + h - 1)
                STT(d_on[:, h % 2], ps[:, 6 + h % 2, T:2 * T], gains[:, 3:4], d_ro[:, h % 2], ALU.mult, ALU.mult).then_inc(da["on"], 1)
                operand_lo(XB, KC * 6 + h + 1, h, d_on[:, h % 2])

            diff_max(0)
            for u in range(2 * DIFF_HEADS):
                h, t = u // 2, u % 2
                if u + 1 < 2 * DIFF_HEADS:
                    diff_max(u + 1)
                st = d_st[:, u % 2]
                nk = (t + 1) * P
                dve.wait_ge(da["p"], u + 1)
                if u >= 2:
                    dve.wait_ge(da["t"], u - 1)
                done(V.reciprocal(st[:, 4:6], st[:, 2:4]))
                TS(st[:, 6:7], st[:, 5:6], d_lam[:, 5:6], None, ALU.mult)
                done(TS(d_a0[:, u % 2, 0:nk], d_p[:, u % 2, 0, 0:nk], st[:, 4:5], None, ALU.mult))
                STT(d_a[:, u % 2, 0:nk], d_p[:, u % 2, 1, 0:nk], st[:, 6:7], d_a0[:, u % 2, 0:nk], ALU.mult, ALU.add).then_inc(da["a"], 1)
                if t == 0 and h:
                    diff_head(h - 1)
            diff_head(DIFF_HEADS - 1)
            residual(C_DO, XA, 3, "mlp_norm1")
            mlp(C_M1, 1, 3, 7, XA, 4, "norm_mix")

            dve.wait_ge(pad_set, 2)
            for b in range(2):
                dve.wait_ge(band_out[b], 16 * (SWA_HEADS // 2))

            def conv_in(i):
                dve.wait_ge(ca["sig"], i + 1)
                TT(c_in[:, i, TAPS - 1:], c_in[:, i, TAPS - 1:], c_tmp[:, i % 2], ALU.mult).then_inc(ca["in"], 1)

            for n in range(16):
                c = C_CONV + n
                i = n // 2
                cut_lo(c + AHEAD, c + AHEAD)
                if n == 0:
                    dve.wait_ge(rstd_done, 5)
                if n % 2 and i >= 2:
                    dve.wait_ge(ca["in"], i - 1)
                scaled(c, c, c_in[:, i, TAPS - 1:] if n % 2 == 0 else c_tmp[:, i % 2])
                if n == 0:
                    dve.wait_ge(sa["dt"], 1)
                    for t in range(NT):
                        at = slice(t * SSD_HEADS, (t + 1) * SSD_HEADS)
                        ins = STT(s_small[:, 0, at], ps[:, 4, at], rtok[:, t:t + 1], pcol("dt_bias", 0, SSD_HEADS), ALU.mult, ALU.add)
                    ins.then_inc(sa["dtx"], 1)
                if n == 1:
                    dve.wait_ge(sa["dta"], 1)
                    done(STT(s_small[:, 5], s_small[:, 0], 0.0, s_small[:, 3], ALU.max, ALU.add))
                    for t in range(NT):
                        at = slice(t * SSD_HEADS, (t + 1) * SSD_HEADS)
                        ins = STT(s_small[:, 6, at], s_small[:, 5, at], -1.0, s_small[:, 4, 0:SSD_HEADS], ALU.mult, ALU.mult)
                    ins.then_inc(sa["da"], 1)
                if n % 2 and i:
                    conv_in(i - 1)
            conv_in(KC - 1)
            for n in range(24):
                c = C_XBC + n
                cut_lo(c + AHEAD, c + AHEAD)
                if n >= 2:
                    dve.wait_ge(sa["silu"], n - 1)
                TT(s_pad[:, n % 2, SSD_TAPS - 1:], got(c, c), rstd[:], ALU.mult).then_inc(bank_free, 1)
                dve.wait_ge(bank_free, c + 1)
                for k in range(SSD_TAPS):
                    w = pcol("ssd_conv_w", n * SSD_TAPS + k)
                    x = s_pad[:, n % 2, k:k + T]
                    if k == 0:
                        TS(s_tap[:, n % 2], x, w, None, ALU.mult).then_inc(sa["tap"], 1)
                    else:
                        dve.wait_ge(sa["tap"], SSD_TAPS * n + k)
                        STT(s_tap[:, n % 2], x, w, s_tap[:, n % 2], ALU.mult, ALU.add).then_inc(sa["tap"], 1)
            with dve.Fori(0, 2) as r:
                for j in range(8):
                    c = C_Z + 8 * r + j
                    cut_lo(c + AHEAD, C_Z + j + AHEAD)
                    scaled(c, C_Z + j, s_z[:, bass.ds(8 * r + j, 1)].rearrange("p o t -> p (o t)"))
            dve.wait_ge(ca["in"], KC)
            for i in range(0, KC, 2):
                for k in range(TAPS):
                    for m in range(2):
                        n = i * TAPS + 2 * k + m
                        x = c_in[:, i + m, k:k + T]
                        if k == 0:
                            TS(c_out[:, i + m], x, pcol("conv_w", (i + m) * TAPS), pcol("conv_b", i + m), ALU.mult, ALU.add).then_inc(ca["tap"], 1)
                        else:
                            dve.wait_ge(ca["tap"], n - 1)
                            STT(c_out[:, i + m], x, pcol("conv_w", (i + m) * TAPS + k), c_out[:, i + m], ALU.mult, ALU.add).then_inc(ca["tap"], 1)
            dve.wait_ge(sa["cs"], 1)
            done(TS(s_small[:, 7], ps[:, 4, 128:128 + NT * SSD_HEADS], -1.0, None, ALU.mult))
            TT(s_small[:, 8, 0:SSD_HEADS], ps[:, 4, 256:256 + SSD_HEADS], s_small[:, 7, 0:SSD_HEADS], ALU.add).then_inc(sa["bias"], 1)
            dve.wait_ge(ca["mean"], 1)
            for k in range(KC):
                ins = STT(c_out[:, k], ps[:, 5, 0:T], -1.0 / D, c_out[:, k], ALU.mult, ALU.add)
            ins.then_inc(ca["xc"], 1)
            dve.wait_ge(ca["r"], 1)
            dve.wait_ge(ca["xc"], 1)
            TT(c_out, c_out, lnt[:, 1].unsqueeze(1).to_broadcast([P, KC, T]), ALU.mult).then_inc(ca["norm"], 1)
            for k in range(KC):
                operand_lo(XB, KC * 11 + k + 1, k, c_out[:, k])

            def gated(c0, branch, n, gate):
                c = c0 + 2 * n
                i = KC * branch + n
                cut_lo(c + AHEAD, c + AHEAD)
                if i >= 2:
                    dve.wait_ge(gate_done, i - 1)
                scaled(c, c, y_tmp[:, n % 2])
                cut_lo(c + 1 + AHEAD, c + 1 + AHEAD)
                dve.wait_ge(gate_done, i + 1)
                into_merged(c + 1, n, gate, branch == 0)

            sums = [0]

            def into_merged(c, n, gate, first):
                if first:
                    TT(merged[:, n], got(c, c), gate, ALU.mult).then_inc(bank_free, 1)
                else:
                    TT(hn_sqb[:, n % 2], got(c, c), gate, ALU.mult).then_inc(bank_free, 1)
                    dve.wait_ge(bank_free, c + 1)
                    TT(merged[:, n], merged[:, n], hn_sqb[:, n % 2], ALU.add).then_inc(merged_done, 1)
                    sums[0] += 1
                    dve.wait_ge(merged_done, sums[0])

            for n in range(KC):
                gated(C_YA, 0, n, y_gate[:, n % 2])

            def ssd_group(g):
                def heads(x, by):
                    return x.rearrange("p (h d) -> p h d", h=8), by.unsqueeze(2).to_broadcast([P, 8, 64])

                for t in range(NT):
                    dve.wait_ge(sa["x"], NT * g + t + 1)
                    at = t * SSD_HEADS + 8 * g
                    x, by = heads(ps[:, 4, :], s_small[:, 5, at:at + 8])
                    TT(s_xd[:, g % 2, t].rearrange("p (h d) -> p h d", h=8), x, by, ALU.mult).then_inc(sa["xd"], 1)
                    if t == 0:
                        dve.wait_ge(sa["xd"], 3 * g + 1)
                        dve.wait_ge(sa["dte"], 1)
                        x, by = heads(s_xd[:, g % 2, 0], s_small[:, 9, 8 * g:8 * g + 8])
                        TT(s_xd2[:, g % 2].rearrange("p (h d) -> p h d", h=8), x, by, ALU.mult).then_inc(sa["xd"], 1)
                for q in range(2):
                    qq = 2 * g + q
                    for t in range(NT):
                        n = qq * NT + t
                        dve.wait_ge(sa["cbs"], g + 1)
                        dve.wait_ge(sa["e"], n + 1)
                        if n >= 2:
                            dve.wait_ge(sa["y"], n // 2)
                        TT(s_sc[:, n % 2].rearrange("p (h l) -> p h l", h=4), s_e[:, n % 2].rearrange("p (h l) -> p h l", h=4),
                           s_cb[:, t].unsqueeze(1).to_broadcast([P, 4, P]), ALU.mult).then_inc(sa["sc"], 1)
                    dve.wait_ge(sa["y"], qq + 1)
                    dve.wait_ge(sa["eb"], qq + 1)
                    for ch in range(2):
                        n = 4 * g + 2 * q + ch
                        STT(s_xbc[:, n], s_xbc[:, n], pcol("ssd_D", n), ps[:, 6, ch * T:(ch + 1) * T], ALU.mult, ALU.add)
                        ins = TT(s_off[:, ch], ps[:, ch, T:T + P], s_eb[:, ch], ALU.mult)
                    done(ins)
                    for ch in range(2):
                        n = 4 * g + 2 * q + ch
                        ins = TT(s_xbc[:, n, P:T], s_xbc[:, n, P:T], s_off[:, ch], ALU.add)
                    done(ins)
                    dve.wait_ge(sa["z"], 16)
                    for ch in range(2):
                        n = 4 * g + 2 * q + ch
                        TT(s_xbc[:, n], s_xbc[:, n], s_z[:, n], ALU.mult).then_inc(sa["yd"], 1)
                dve.wait_ge(sa["r"], g + 1)
                for k in range(4):
                    n = 4 * g + k
                    STT(s_xbc[:, n], s_xbc[:, n], pcol("ssd_norm", n), s_rg[:], ALU.mult, ALU.mult).then_inc(sa["on"], 1)
                for k in range(4):
                    operand_lo(XB, KC * 12 + 4 * g + k + 1, 4 * (g % 2) + k, s_xbc[:, 4 * g + k])

            ssd_group(0)
            ssd_group(1)
            for n in range(KC):
                gated(C_YB0, 1, n, gate_b[:, n])
            ssd_group(2)
            ssd_group(3)
            for n in range(KC):
                cut_lo(C_YB1 + n + AHEAD, C_YB1 + n + AHEAD)
                into_merged(C_YB1 + n, n, gate_b[:, n], False)

            for n in range(12):
                c = C_SWA + n
                if n < 10:
                    cut_lo(c + AHEAD, c + AHEAD)
                    scaled(c, c, w_q[:, n] if n < 8 else w_k2[:, n - 8])
                if n >= 2:
                    i = n - 2
                    head_out(16 + i, w_q[:, i] if i < 8 else w_k2[:, i - 8], pcol("swa_q_norm" if i < 8 else "swa_k_norm"))
            for n in range(10, 12):
                c = C_SWA + n
                cut_lo(c + AHEAD, c + AHEAD)
                tokens(c, c, w_v[:, :, (n - 10) * P:(n - 9) * P], rtok)

            def swa_max(u):
                p, t = u // 2, u % 2
                nk = (t + 1) * P
                st = w_st[:, u % 2]
                dve.wait_ge(wa["s"], u + 1)
                dve.wait_ge(band_in[u % 2], 16 * (u // 2 + 1))
                if u >= 2:
                    dve.wait_ge(wa["p"], u - 1)
                STT(w_s[:, u % 2, :, 0:nk], swa_scores_at(u)[:, :, 0:nk], float(SWA_DH) ** -0.5,
                    w_bias[:, u % 2, :, 0:nk], ALU.mult, ALU.add).then_inc(wa["ss"], 1)
                dve.wait_ge(wa["ss"], u + 1)
                done(V.tensor_reduce(st[:, 0:2], w_s[:, u % 2, :, 0:nk], AX.X, ALU.max))
                done(TT(st[:, 0:2], st[:, 0:2], pcol("sinks", 2 * p, 2), ALU.max))
                done(TS(st[:, 2:4], st[:, 0:2], -1.0, None, ALU.mult))
                TT(st[:, 6:8], st[:, 2:4], pcol("sinks", 2 * p, 2), ALU.add).then_inc(wa["m"], 1)

            def swa_lo(p):
                dve.wait_ge(XB.bf_done, KC * 14 + p + 1)
                operand_lo(XB, KC * 14 + p + 1, p, ps[:, OUT_BANKS[p % 2], 0:T])

            swa_max(0)
            for u in range(2 * SWA_PAIRS):
                p, t = u // 2, u % 2
                if u + 1 < 2 * SWA_PAIRS:
                    swa_max(u + 1)
                st = w_st[:, u % 2]
                dve.wait_ge(wa["p"], u + 1)
                done(TT(st[:, 10:12], st[:, 4:6], st[:, 8:10], ALU.add))
                done(V.reciprocal(st[:, 12:14], st[:, 10:12]))
                for i in range(2):
                    x = w_p[:, u % 2, i, 0:(t + 1) * P]
                    ins = TS(x, x, st[:, 12 + i:13 + i], None, ALU.mult)
                ins.then_inc(wa["r"], 1)
                if t == 0 and p:
                    swa_lo(p - 1)
            swa_lo(SWA_PAIRS - 1)
            for n in range(KC):
                gated(C_YC, 2, n, y_gate[:, n % 2])
            for k in range(KC):
                operand_lo(XB, KC * 15 + k + 1, k, merged[:, k])
            for k in range(KC):
                operand_lo(XA, KC * 5 + k + 1, k, x_mem[:, k], pcol("norm_mem", k))
            residual(C_MIX, None, None, None)
            for k in range(KC):
                operand_lo(XB, KC * 16 + k + 1, k, H[:, k], pcol("norm_xattn", k))

            def pair_out(k, x, gain):
                dve.wait_ge(xa["r"], k + 1)
                for i in range(2):
                    STT(x[:, i], x[:, i], gain[:, i:i + 1], x_rk[:, k % 2], ALU.mult, ALU.mult).then_inc(xa["out"], 1)

            for n in range(12):
                if n < 8:
                    c = C_XK + n
                    cut_lo(c + AHEAD, c + AHEAD)
                    if n == 0:
                        dve.wait_ge(rstd_done, 6)
                    TT(x_k[:, n], got(c, c), rstd_mem[:], ALU.mult).then_inc(bank_free, 1)
                if n >= 4 and n % 2 == 0:
                    k = n // 2 - 2
                    pair_out(k, x_k[:, 2 * k:2 * k + 2], pcol("xk_norm", 0, 2))
            for n in range(8):
                c = C_XV + n
                cut_lo(c + AHEAD, c + AHEAD)
                tokens(c, c, x_v[:, :, n * P:(n + 1) * P], rtok_mem)
            for n in range(12):
                if n < 8:
                    c = C_XQ + n
                    cut_lo(c + AHEAD, c + AHEAD)
                    if n == 0:
                        dve.wait_ge(rstd_done, 7)
                    scaled(c, c, x_q[:, n])
                if n >= 4 and n % 2 == 0:
                    k = n // 2 - 2
                    pair_out(4 + k, x_q[:, 2 * k:2 * k + 2], gains[:, 0:2])

            def x_max(h):
                dve.wait_ge(xa["s"], h + 1)
                V.tensor_reduce(x_st[:, h % 2, 0:2], ps[:, 4 + h % 2, :].rearrange("p (c k) -> p c k", c=2), AX.X, ALU.max,
                                negate=True).then_inc(xa["max"], 1)

            def x_lo(h):
                dve.wait_ge(XB.bf_done, KC * 17 + 2 * h + 2)
                for half in range(2):
                    operand_lo(XB, KC * 17 + 2 * h + half + 1, 2 * h + half, ps[:, OUT_BANKS[h % 2], half * T:(half + 1) * T])

            x_max(0)
            for h in range(X_HEADS):
                if h + 1 < X_HEADS:
                    x_max(h + 1)
                st = x_st[:, h % 2]
                dve.wait_ge(xa["p"], h + 1)
                done(V.reciprocal(st[:, 4:6], st[:, 2:4]))
                for t in range(NT):
                    ins = TS(x_p[:, h % 2, t], x_p[:, h % 2, t], st[:, 4 + t:5 + t], None, ALU.mult)
                ins.then_inc(xa["n"], 1)
                if h:
                    x_lo(h - 1)
            x_lo(X_HEADS - 1)
            residual(C_XO, XA, 6, "norm_mlp2")
            mlp(C_M2, 2, 7, 18, None, None, None)

        @block.gpsimd
        def _(pool):
            G = nc.gpsimd
            steps = [0]

            def sum_squares(nu, src, ready, base):
                for k in range(KC):
                    pool.wait_ge(ready, base(k))
                    if k == 0:
                        if nu:
                            pool.wait_ge(stat_mm, nu)
                        G.tensor_tensor(sumsq[:], src[:, k], src[:, k], ALU.mult).then_inc(sq_step, 1)
                        steps[0] += 1
                    else:
                        pool.wait_ge(sq_step, steps[0])
                        G.tensor_tensor(sqtmp[:], src[:, k], src[:, k], ALU.mult).then_inc(sq_step, 1)
                        steps[0] += 1
                        pool.wait_ge(sq_step, steps[0])
                        G.tensor_tensor(sumsq[:], sumsq[:], sqtmp[:], ALU.add).then_inc(sq_step, 1)
                        steps[0] += 1

            def residual_squares(nu, c0):
                sum_squares(nu, H, bank_free, lambda k: c0 + k + 1)

            def mlp(c0, m, xb_build0):
                def group(g):
                    for j in range(8):
                        pool.wait_ge(bank_free, c0 + 16 * g + j + 1)
                        pool.wait_ge(XB.lo_done, KC * (xb_build0 + g) + j - 1)
                        pool.wait_ge(XB.bf_done, KC * (xb_build0 + g) + j - 1)
                        G.tensor_tensor(m_sq[:, j % 2], m_relu[:, j % 2], m_relu[:, j % 2], ALU.mult).then_inc(sq_done, 1)
                with pool.Fori(0, HID_GROUPS) as g:
                    group(g)

            G.memset(ones[:], 1.0)
            G.memset(eps[:], EPS)
            G.memset(one[:], 1.0).then_inc(set_done, 1)
            G.memset(g_z, 1.0).then_inc(ga["zs"], 1)
            sum_squares(0, H, in_done, lambda k: 16)
            residual_squares(1, C_GO)
            mlp(C_M0, 0, 1)
            residual_squares(2, C_M0 + 56)
            for h in range(SWA_HEADS):
                pool.wait_ge(band_set, h + 1)
                pool.dma_start(band_d[:, h], w_row[:, h % 2]).then_inc(band_out[h % 2], 16)
            residual_squares(3, C_DO)
            mlp(C_M1, 1, 7)
            residual_squares(4, C_M1 + 56)
            G.memset(c_in[:, :, 0:TAPS - 1], 0.0).then_inc(pad_set, 1)
            G.memset(s_pad[:, :, 0:SSD_TAPS - 1], 0.0).then_inc(pad_set, 1)
            pool.wait_ge(bank_free, C_SWA)
            pool.dma_start(x_mem, mem_d).then_inc(mem_in, 16)
            for b in range(2):
                pool.wait_ge(band_out[b], 16 * (SWA_HEADS // 2))
            for u in range(2 * SWA_PAIRS):
                p, t = u // 2, u % 2
                nk = (t + 1) * P
                if u >= 2:
                    pool.wait_ge(wa["ss"], u - 1)
                skew = bass.AP(band_d.tensor, 2 * p * BAND + P - 1 + (1 - t) * P, [[SWA_HEADS * BAND - 1, P], [BAND, 2], [1, nk]])
                pool.dma_start(w_bias[:, u % 2, :, 0:nk], skew).then_inc(band_in[u % 2], 16)
            sum_squares(5, x_mem, mem_in, lambda k: 16)
            residual_squares(6, C_MIX)
            residual_squares(7, C_XO)
            mlp(C_M2, 2, 18)


def constants():
    i = np.arange(P)
    con = np.zeros((P, NCON), np.float32)

    def put(name, a):
        con[0:a.shape[0], CCOL[name]:CCOL[name] + a.shape[1]] = a

    put("ident", np.eye(P))
    put("bones", i[:, None] // 64 == i[None, :] // 64)
    put("upto", i[:, None] <= i[None, :])
    put("after", i[None, :] > i[:, None])
    dist = 2 * P - 1 - np.arange(BAND)
    large = 16 + (np.log(np.maximum(dist, 1).astype(np.float32) / np.float32(16)) / np.log(np.float32(8)) * np.float32(16)).astype(np.int32)
    bucket = np.where(dist < 16, np.maximum(dist, 0), np.minimum(large, 31))
    inside = (dist >= 0) & (dist < P)
    oh = np.zeros((33, BAND), np.float32)
    oh[bucket[inside], np.nonzero(inside)[0]] = 1.0
    oh[32, ~inside] = NEG
    put("oh", oh)
    j, t = i[:, None], i[None, :]
    ranges = [j > t]
    pairs = []
    for lv in range(LEVELS):
        half = 1 << lv
        mid = t // (2 * half) * 2 * half + half - 1
        ranges.append(np.where(t > mid, (j > mid) & (j <= t), (j > t) & (j <= mid)))
        same = j // (2 * half) == t // (2 * half)
        pairs.append(same & (j % (2 * half) < half) & (t % (2 * half) >= half))
    ranges.append(j <= t)
    pairs.append(j == t)
    return con, np.concatenate(ranges + pairs, 1).astype(np.float32)


def columns(v):
    return v.reshape(-1, P).T


def stream(x):
    def cut(w):
        w = np.asarray(w)
        return [w[:, n * P:(n + 1) * P] for n in range(w.shape[1] // P)]

    def mlp(w1, w2):
        up, out = cut(w1), []
        for g in range(HID_GROUPS):
            out += up[8 * g:8 * g + 8] + cut(w2[g * D:(g + 1) * D])
        return out

    def turns(a, b):
        return [c for pair in zip(a, b) for c in pair]

    a, b = x["a_w_in"][0], x["w_in_2"][0]
    gates = cut(b[:, 8736:11808])
    conv = cut(b[:, 0:2048])
    ssd = x["w_ssd_out_2"][0]
    out = cut(a[:, 0:3072]) + cut(x["a_w_out"][0]) + mlp(x["mlp_w1"][0], x["mlp_w2"][0])
    out += cut(x["w_kv"]) + cut(x["b_w_q"][0]) + cut(x["b_w_out"][0]) + mlp(x["mlp_w1"][1], x["mlp_w2"][1])
    out += turns(conv[0:8], conv[8:16]) + cut(b[:, 4096:7168]) + cut(b[:, 2048:4096])
    out += turns(gates[0:8], cut(x["w_conv_out_2"][0])) + turns(gates[8:16], cut(ssd[0:D])) + cut(ssd[D:])
    out += cut(b[:, 7200:8736]) + turns(gates[16:24], cut(x["w_attn_out_2"][0])) + cut(x["w_mix_out_2"][0])
    out += cut(x["w_xkv_2"][0]) + cut(x["w_xq_2"][0]) + cut(x["w_xo_2"][0]) + mlp(x["w_mlp_up_2"][0], x["w_mlp_down_2"][0])
    assert len(out) == CHUNKS
    w = np.empty((SLABS, P, 2, KC, P), np.float32)
    for n, c in enumerate(out):
        w[n // 2, :, n % 2] = c.reshape(KC, P, P).transpose(1, 0, 2)
    return w.reshape(SLABS, P, 2 * D)


def parameters(x):
    par = np.zeros((P, NPAR), np.float32)

    def put(name, a):
        a = np.asarray(a)
        par[0:a.shape[0], PCOL[name]:PCOL[name] + a.shape[1]] = a

    def twice(v):
        return np.concatenate([v, v])[:, None]

    def rows(v):
        return np.broadcast_to(np.asarray(v).reshape(1, -1), (P, np.size(v)))

    b = x["w_in_2"][0]
    for name, v in (
        ("a_norm", x["a_norm"][0]), ("a_head_norm", x["a_head_norm"][0]), ("kv_norm", x["kv_norm"]), ("b_norm", x["b_norm"][0]),
        ("mlp_norm0", x["mlp_norm"][0]), ("mlp_norm1", x["mlp_norm"][1]), ("b_head_norm", x["b_head_norm"][0]),
        ("norm_mix", x["norm_mix_2"][0]), ("conv_b", x["conv_dw_b_2"][0]), ("ln_g", x["conv_ln_g_2"][0]), ("ln_b", x["conv_ln_b_2"][0]),
        ("ssd_conv_b", x["ssd_conv_b_2"][0]), ("ssd_norm", x["ssd_norm_g_2"][0]), ("gate_bias", x["gate_bias_2"][0].reshape(-1)),
        ("norm_xattn", x["norm_xattn_2"][0]), ("norm_mem", x["norm_mem_2"][0]), ("xq_norm", x["xattn_q_norm_2"][0]),
        ("xk_norm", x["xattn_k_norm_2"][0]), ("norm_mlp2", x["norm_mlp_2"][0]), ("ssd_D", np.repeat(x["ssd_D_2"][0], 64)),
    ):
        put(name, columns(v))
    for name, v in (("k_norm", x["k_norm"]), ("b_q_norm", x["b_q_norm"][0]), ("swa_q_norm", x["attn_q_norm_2"][0]),
                    ("swa_k_norm", x["attn_k_norm_2"][0])):
        put(name, twice(v))
    for name, v in (("dt_bias", x["ssd_dt_bias_2"][0]), ("A_log", x["ssd_A_log_2"][0]), ("sinks", x["attn_sinks_2"][0]),
                    ("b_lambda", x["b_lambda"][0])):
        put(name, rows(v))
    put("conv_w", x["conv_dw_w_2"][0].reshape(TAPS, KC, P).transpose(2, 1, 0).reshape(P, -1))
    put("ssd_conv_w", x["ssd_conv_w_2"][0].reshape(SSD_TAPS, 24, P).transpose(2, 1, 0).reshape(P, -1))
    put("w_z", x["a_w_in"][0][:, 3072:3088].reshape(KC, P, GLA_RANK).transpose(1, 0, 2).reshape(P, -1))
    put("w_dt", b[:, 7168:7200].reshape(KC, P, SSD_HEADS).transpose(1, 0, 2).reshape(P, -1))
    put("gate_up", np.concatenate([x["a_w_gate_up"][0], x["a_b_gate"]]))
    put("rel", np.concatenate([x["rel_table_2"], np.ones((1, SWA_HEADS), np.float32)]))
    return par


def kernel(**inputs):
    import concourse.bacc as bacc
    from concourse.bass_utils import run_bass_kernel_spmd

    x = {k: np.asarray(v) for k, v in inputs.items()}
    con, masks = constants()
    arrays = {
        "weights": stream(x),
        "params": parameters(x),
        "consts": con,
        "gla_masks": masks,
        "x_t": np.ascontiguousarray(x["x"][0].T.reshape(KC, P, T).transpose(1, 0, 2)),
        "mem_t": np.ascontiguousarray(x["mem_2"][0].T.reshape(KC, P, T).transpose(1, 0, 2)),
    }
    nc = bacc.Bacc("TRN2", target_bir_lowering=False, num_devices=1)
    args = [nc.dram_tensor(n, a.shape, F32, kind="ExternalInput").ap() for n, a in arrays.items()]
    band = nc.dram_tensor("band", (P, SWA_HEADS, BAND), F32, kind="Internal").ap()
    out = nc.dram_tensor("out_t", (P, KC, T), F32, kind="ExternalOutput").ap()
    program(nc, *args, band, out)
    r = run_bass_kernel_spmd(nc, [arrays], core_ids=[0])
    return np.ascontiguousarray(r.results[0]["out_t"].transpose(1, 0, 2).reshape(D, T).T).reshape(1, T, D)
```
